# Optimizing a Trainium2 kernel written in Bass

```python
import math
import jax, jax.numpy as jnp
from jax import lax
import numpy as np

D_MODEL = 2048
BATCH = 1
SEQ = 256
DEPTH = 1

H_A = 8
DQK_A = 128
DV_A = 256
D_A = H_A * DV_A
QK_A = H_A * DQK_A
CHUNK = 64
CONV_K = 4
H_B = 16
D_NOPE = 128
D_ROPE = 64
D_HQK = D_NOPE + D_ROPE
D_VB = 128
D_B = H_B * D_VB
Q_LORA = 512
KV_LORA = 512
Q_BLOCK = 128
ROPE_THETA = 10000.0
EPS = 1e-6
NEG_INF = -1e30
SPLIT_SIZES = (QK_A, QK_A, D_A, D_A, H_A, H_A, D_A, Q_LORA, KV_LORA, D_ROPE, D_B, D_MODEL, D_MODEL)
N_IN = sum(SPLIT_SIZES)


def rms_norm(x, g):
    x32 = x.astype(jnp.float32)
    y = x32 * lax.rsqrt(jnp.mean(x32 * x32, axis=-1, keepdims=True) + EPS)
    return (y * g.astype(jnp.float32)).astype(x.dtype)

def causal_depthwise_conv(x, w):
    s_len = x.shape[1]
    xp = jnp.pad(x, ((0, 0), (CONV_K - 1, 0), (0, 0)))
    out = xp[:, CONV_K - 1:] * w[CONV_K - 1]
    for j in range(CONV_K - 1):
        out = out + xp[:, j:j + s_len] * w[j]
    return out

def rope_tables(positions):
    inv_freq = jnp.exp(-math.log(ROPE_THETA) * jnp.arange(0, D_ROPE, 2, dtype=jnp.float32) / D_ROPE)
    ang = positions.astype(jnp.float32)[..., None] * inv_freq
    return jnp.cos(ang)[:, :, None, :], jnp.sin(ang)[:, :, None, :]

def apply_rope(x, cos, sin):
    x32 = x.astype(jnp.float32)
    x1, x2 = jnp.split(x32, 2, axis=-1)
    return jnp.concatenate([x1 * cos - x2 * sin, x2 * cos + x1 * sin], axis=-1).astype(x.dtype)

def mlstm_chunkwise(q, k, v, i_pre, f_pre):
    b_sz, s_len, n_h, dk = q.shape
    dv = v.shape[-1]
    n_chunks = s_len // CHUNK
    f32 = jnp.float32

    def chunks(t):
        t = t.astype(f32).reshape((b_sz, n_chunks, CHUNK, n_h) + t.shape[3:])
        return jnp.moveaxis(t, (1, 3), (0, 2))

    qc_all = chunks(q) * (dk ** -0.5)
    kc_all = chunks(k)
    vc_all = chunks(v)
    ic_all = chunks(i_pre)
    lf_all = jax.nn.log_sigmoid(chunks(f_pre))
    causal = jnp.tril(jnp.ones((CHUNK, CHUNK), dtype=bool))

    def step(carry, xs):
        c_st, n_st, m_st = carry
        qc, kc, vc, ic, fc = xs
        b = jnp.cumsum(fc, axis=-1)
        g = b[..., -1]
        d = jnp.where(causal, b[..., :, None] - b[..., None, :] + ic[..., None, :], NEG_INF)
        inter = b + m_st[..., None]
        m_i = jnp.maximum(jnp.max(d, axis=-1), inter)
        s = jnp.einsum('bhid,bhjd->bhij', qc, kc) * jnp.exp(d - m_i[..., None])
        decay = jnp.exp(inter - m_i)
        num = jnp.einsum('bhij,bhje->bhie', s, vc) + decay[..., None] * jnp.einsum('bhid,bhde->bhie', qc, c_st)
        den = jnp.sum(s, axis=-1) + decay * jnp.einsum('bhid,bhd->bhi', qc, n_st)
        h = num / jnp.maximum(jnp.abs(den), jnp.exp(-m_i))[..., None]
        w = g[..., None] - b + ic
        m_new = jnp.maximum(g + m_st, jnp.max(w, axis=-1))
        carry_scale = jnp.exp(g + m_st - m_new)
        kw = kc * jnp.exp(w - m_new[..., None])[..., None]
        c_new = carry_scale[..., None, None] * c_st + jnp.einsum('bhjd,bhje->bhde', kw, vc)
        n_new = carry_scale[..., None] * n_st + jnp.sum(kw, axis=-2)
        return (c_new, n_new, m_new), h

    init = (jnp.zeros((b_sz, n_h, dk, dv), f32), jnp.zeros((b_sz, n_h, dk), f32), jnp.zeros((b_sz, n_h), f32))
    _, h_all = lax.scan(step, init, (qc_all, kc_all, vc_all, ic_all, lf_all))
    h_all = jnp.moveaxis(h_all, (0, 2), (1, 3)).reshape(b_sz, s_len, n_h, dv)
    return h_all.astype(v.dtype)

def causal_attention(q, k, v):
    b_sz, s_len, n_h, dq = q.shape
    n_blocks = s_len // Q_BLOCK
    scale = dq ** -0.5
    key_idx = jnp.arange(s_len)
    q_blocks = jnp.moveaxis(q.reshape(b_sz, n_blocks, Q_BLOCK, n_h, dq), 1, 0)

    def one_block(args):
        q_blk, blk_id = args
        q_idx = blk_id * Q_BLOCK + jnp.arange(Q_BLOCK)
        s = jnp.einsum('bqhd,bkhd->bhqk', q_blk, k).astype(jnp.float32) * scale
        s = jnp.where(key_idx[None, :] <= q_idx[:, None], s, NEG_INF)
        p = jax.nn.softmax(s, axis=-1).astype(v.dtype)
        return jnp.einsum('bhqk,bkhd->bqhd', p, v)

    o = lax.map(one_block, (q_blocks, jnp.arange(n_blocks)))
    return jnp.moveaxis(o, 0, 1).reshape(b_sz, s_len, n_h, v.shape[-1])

def hybrid_layer(x, cos, sin, norm_g, w_in, gate_bias, conv_w, mlstm_norm_g, w_a,
                 q_lat_g, kv_lat_g, w_uq, w_ukv, q_norm_g, k_norm_g, w_b, w_out):
    b_sz, s_len, _ = x.shape
    h = rms_norm(x, norm_g)
    proj = jnp.einsum('bsd,dn->bsn', h, w_in)
    offsets = [int(o) for o in np.cumsum(SPLIT_SIZES)[:-1]]
    (q_a, k_a, v_a, o_a, i_a, f_a, z_a, c_q, c_kv, k_r, z_b, g_a, g_b) = jnp.split(proj, offsets, axis=-1)

    qk_a = jax.nn.silu(causal_depthwise_conv(jnp.concatenate([q_a, k_a], axis=-1), conv_w))
    q_a, k_a = jnp.split(qk_a, 2, axis=-1)
    h_a = mlstm_chunkwise(q_a.reshape(b_sz, s_len, H_A, DQK_A),
                          k_a.reshape(b_sz, s_len, H_A, DQK_A),
                          v_a.reshape(b_sz, s_len, H_A, DV_A),
                          i_a + gate_bias[:H_A], f_a + gate_bias[H_A:])
    h_a = rms_norm(h_a, mlstm_norm_g.reshape(H_A, DV_A)).reshape(b_sz, s_len, D_A)
    y_a = jnp.einsum('bsc,cd->bsd', jax.nn.sigmoid(o_a) * h_a * jax.nn.silu(z_a), w_a)

    q_b = jnp.einsum('bsr,rn->bsn', rms_norm(c_q, q_lat_g), w_uq).reshape(b_sz, s_len, H_B, D_HQK)
    kv_b = jnp.einsum('bsr,rn->bsn', rms_norm(c_kv, kv_lat_g), w_ukv).reshape(b_sz, s_len, H_B, D_NOPE + D_VB)
    k_nope, v_b = jnp.split(kv_b, [D_NOPE], axis=-1)
    k_b = jnp.concatenate([k_nope, jnp.broadcast_to(k_r[:, :, None, :], (b_sz, s_len, H_B, D_ROPE))], axis=-1)
    q_b = rms_norm(q_b, q_norm_g)
    k_b = rms_norm(k_b, k_norm_g)
    q_b = jnp.concatenate([q_b[..., :D_NOPE], apply_rope(q_b[..., D_NOPE:], cos, sin)], axis=-1)
    k_b = jnp.concatenate([k_b[..., :D_NOPE], apply_rope(k_b[..., D_NOPE:], cos, sin)], axis=-1)
    o_b = causal_attention(q_b, k_b, v_b).reshape(b_sz, s_len, D_B)
    y_b = jnp.einsum('bsc,cd->bsd', o_b * jax.nn.silu(z_b), w_b)

    y = jax.nn.sigmoid(g_a) * y_a + jax.nn.sigmoid(g_b) * y_b
    return x + jnp.einsum('bsd,de->bse', y, w_out)

def first_inputs(seed: int = 0) -> dict:
    key = jax.random.key(seed)
    ks = jax.random.split(key, 16)
    f32 = jnp.float32

    def nrm(k, shape, scale):
        return jax.random.normal(k, shape, f32) * scale

    x = nrm(ks[0], (BATCH, SEQ, D_MODEL), 1.0)
    positions = (jax.random.randint(ks[1], (BATCH, 1), 0, 1024, dtype=jnp.int32)
                 + jnp.arange(SEQ, dtype=jnp.int32)[None, :])
    norm_g = 1.0 + nrm(ks[2], (DEPTH, D_MODEL), 0.02)
    w_in = nrm(ks[3], (DEPTH, D_MODEL, N_IN), D_MODEL ** -0.5)
    kb1, kb2 = jax.random.split(ks[4])
    gate_bias = jnp.concatenate([nrm(kb1, (DEPTH, H_A), 0.1),
                                 jnp.linspace(3.0, 6.0, H_A, dtype=f32)[None, :] + nrm(kb2, (DEPTH, H_A), 0.1)], axis=-1)
    conv_w = nrm(ks[5], (DEPTH, CONV_K, 2 * QK_A), CONV_K ** -0.5)
    mlstm_norm_g = 1.0 + nrm(ks[6], (DEPTH, D_A), 0.02)
    w_a = nrm(ks[7], (DEPTH, D_A, D_MODEL), D_A ** -0.5)
    q_lat_g = 1.0 + nrm(ks[8], (DEPTH, Q_LORA), 0.02)
    kv_lat_g = 1.0 + nrm(ks[9], (DEPTH, KV_LORA), 0.02)
    w_uq = nrm(ks[10], (DEPTH, Q_LORA, H_B * D_HQK), Q_LORA ** -0.5)
    w_ukv = nrm(ks[11], (DEPTH, KV_LORA, H_B * (D_NOPE + D_VB)), KV_LORA ** -0.5)
    q_norm_g = 1.0 + nrm(ks[12], (DEPTH, D_HQK), 0.02)
    k_norm_g = 1.0 + nrm(ks[13], (DEPTH, D_HQK), 0.02)
    w_b = nrm(ks[14], (DEPTH, D_B, D_MODEL), D_B ** -0.5)
    w_out = nrm(ks[15], (DEPTH, D_MODEL, D_MODEL), D_MODEL ** -0.5)
    return {"x": x, "positions": positions, "norm_g": norm_g, "w_in": w_in, "gate_bias": gate_bias,
            "conv_w": conv_w, "mlstm_norm_g": mlstm_norm_g, "w_a": w_a, "q_lat_g": q_lat_g,
            "kv_lat_g": kv_lat_g, "w_uq": w_uq, "w_ukv": w_ukv, "q_norm_g": q_norm_g,
            "k_norm_g": k_norm_g, "w_b": w_b, "w_out": w_out}

def first_block(x, positions, norm_g, w_in, gate_bias, conv_w, mlstm_norm_g, w_a, q_lat_g,
              kv_lat_g, w_uq, w_ukv, q_norm_g, k_norm_g, w_b, w_out):
    cos, sin = rope_tables(positions)
    for l in range(DEPTH):
        x = hybrid_layer(x, cos, sin, norm_g[l], w_in[l], gate_bias[l], conv_w[l], mlstm_norm_g[l],
                         w_a[l], q_lat_g[l], kv_lat_g[l], w_uq[l], w_ukv[l], q_norm_g[l],
                         k_norm_g[l], w_b[l], w_out[l])
    return x


MIX_WIDTH = D_MODEL
FOURIER_WIDTH = MIX_WIDTH // 2
N_FOURIER_GROUPS = 4
FOURIER_GROUP_DIM = FOURIER_WIDTH // N_FOURIER_GROUPS
ATTN_WIDTH = MIX_WIDTH - FOURIER_WIDTH
HEAD_DIM = 128
N_HEADS = ATTN_WIDTH // HEAD_DIM
WINDOW_DILATIONS = ((128, 1), (512, 4), (2048, 16))
D_FF = 4 * D_MODEL
IN_WIDTH = FOURIER_WIDTH + 3 * ATTN_WIDTH
RMS_EPS = 1e-6


def _rmsnorm(x, g):
    xf = x.astype(jnp.float32)
    inv = lax.rsqrt(jnp.mean(xf * xf, axis=-1, keepdims=True) + RMS_EPS)
    return (xf * inv * g.astype(jnp.float32)).astype(x.dtype)

def _alibi_slopes(n_heads):
    return jnp.asarray(2.0 ** (-8.0 * (np.arange(n_heads) + 1) / n_heads), dtype=jnp.float32)

def _dilated_branch(q, k, v, slopes, dilation, radius):
    B, H, S, Dh = q.shape
    M = S // dilation
    blk = radius
    nb = -(-M // blk)
    Mp = nb * blk

    def to_classes(t):
        return t.reshape(B, H, M, dilation, Dh).transpose(0, 1, 3, 2, 4)

    pad0 = ((0, 0), (0, 0), (0, 0))
    qc = jnp.pad(to_classes(q), pad0 + ((0, Mp - M), (0, 0))).reshape(B, H, dilation, nb, blk, Dh)
    kc = jnp.pad(to_classes(k), pad0 + ((blk, Mp - M + blk), (0, 0))).reshape(B, H, dilation, nb + 2, blk, Dh)
    vc = jnp.pad(to_classes(v), pad0 + ((blk, Mp - M + blk), (0, 0))).reshape(B, H, dilation, nb + 2, blk, Dh)
    kw = jnp.concatenate([kc[:, :, :, :-2], kc[:, :, :, 1:-1], kc[:, :, :, 2:]], axis=4)
    vw = jnp.concatenate([vc[:, :, :, :-2], vc[:, :, :, 1:-1], vc[:, :, :, 2:]], axis=4)

    mq = jnp.arange(nb)[:, None, None] * blk + jnp.arange(blk)[None, :, None]
    mk = jnp.arange(nb)[:, None, None] * blk - blk + jnp.arange(3 * blk)[None, None, :]
    rel = mk - mq
    valid = (jnp.abs(rel) <= radius) & (mk >= 0) & (mk < M)
    dist = (dilation * jnp.abs(rel)).astype(jnp.float32)

    s = jnp.einsum('bhrnqd,bhrnkd->bhrnqk', qc, kw).astype(jnp.float32)
    s = s - slopes[None, :, None, None, None, None] * dist
    s = jnp.where(valid, s, -jnp.inf)
    mx = jnp.max(s, axis=-1, keepdims=True)
    p = jnp.exp(s - mx)
    den = jnp.sum(p, axis=-1)
    o = jnp.einsum('bhrnqk,bhrnkd->bhrnqd', p.astype(v.dtype), vw).astype(jnp.float32) / den[..., None]

    def from_classes(t):
        tail = t.shape[5:]
        t = t.reshape((B, H, dilation, Mp) + tail)[:, :, :, :M]
        t = jnp.moveaxis(t, 2, 3)
        return t.reshape((B, H, S) + tail)

    return from_classes(o), from_classes(mx[..., 0]), from_classes(den)

def _dilated_attention(q, k, v):
    slopes = _alibi_slopes(q.shape[1])
    outs, maxes, dens = [], [], []
    for window, dil in WINDOW_DILATIONS:
        o, m, d = _dilated_branch(q, k, v, slopes, dil, (window // 2) // dil)
        outs.append(o); maxes.append(m); dens.append(d)
    mx = jnp.stack(maxes)
    w = jnp.stack(dens) * jnp.exp(mx - jnp.max(mx, axis=0, keepdims=True))
    o = jnp.sum(w[..., None] * jnp.stack(outs), axis=0) / jnp.sum(w, axis=0)[..., None]
    return o

def _fourier_mix(u, w_f):
    B, S, _ = u.shape
    ug = u.reshape(B, S, N_FOURIER_GROUPS, FOURIER_GROUP_DIM).astype(jnp.float32)
    re = jnp.fft.fft2(ug, axes=(1, 3), norm="ortho").real.astype(u.dtype)
    y = jnp.einsum('bsgc,gce->bsge', re, w_f)
    return y.reshape(B, S, FOURIER_WIDTH)

def second_inputs(seed: int = 0) -> dict:
    key = jax.random.key(seed)
    ks = jax.random.split(key, 10)
    f32 = jnp.float32
    x = jax.random.normal(ks[0], (BATCH, SEQ, D_MODEL), f32)
    norm_mix_g = 1.0 + 0.02 * jax.random.normal(ks[1], (DEPTH, D_MODEL), f32)
    w_in = jax.random.normal(ks[2], (DEPTH, D_MODEL, IN_WIDTH), f32) * D_MODEL ** -0.5
    w_fourier = jax.random.normal(ks[3], (DEPTH, N_FOURIER_GROUPS, FOURIER_GROUP_DIM, FOURIER_GROUP_DIM), f32) * FOURIER_GROUP_DIM ** -0.5
    w_out = jax.random.normal(ks[4], (DEPTH, MIX_WIDTH, D_MODEL), f32) * MIX_WIDTH ** -0.5
    norm_mlp_g = 1.0 + 0.02 * jax.random.normal(ks[5], (DEPTH, D_MODEL), f32)
    w_up = jax.random.normal(ks[6], (DEPTH, D_MODEL, D_FF), f32) * D_MODEL ** -0.5
    w_down = jax.random.normal(ks[7], (DEPTH, D_FF, D_MODEL), f32) * D_FF ** -0.5
    norm_final_g = 1.0 + 0.02 * jax.random.normal(ks[8], (D_MODEL,), f32)
    return {"x": x, "norm_mix_g": norm_mix_g, "w_in": w_in, "w_fourier": w_fourier,
            "w_out": w_out, "norm_mlp_g": norm_mlp_g, "w_up": w_up, "w_down": w_down,
            "norm_final_g": norm_final_g}

def second_block(x, norm_mix_g, w_in, w_fourier, w_out, norm_mlp_g, w_up, w_down, norm_final_g):
    B, S, _ = x.shape
    h = x
    for layer in range(DEPTH):
        u = _rmsnorm(h, norm_mix_g[layer])
        proj = jnp.einsum('bsd,de->bse', u, w_in[layer])
        u_f = proj[..., :FOURIER_WIDTH]
        qkv = proj[..., FOURIER_WIDTH:].reshape(B, S, 3, N_HEADS, HEAD_DIM)
        q = jnp.transpose(qkv[:, :, 0], (0, 2, 1, 3)) * (HEAD_DIM ** -0.5)
        k = jnp.transpose(qkv[:, :, 1], (0, 2, 1, 3))
        v = jnp.transpose(qkv[:, :, 2], (0, 2, 1, 3))
        y_f = _fourier_mix(u_f, w_fourier[layer])
        y_a = _dilated_attention(q, k, v).astype(h.dtype)
        y_a = jnp.transpose(y_a, (0, 2, 1, 3)).reshape(B, S, ATTN_WIDTH)
        y = jnp.concatenate([y_f, y_a], axis=-1)
        h = h + jnp.einsum('bse,ed->bsd', y, w_out[layer])
        u = _rmsnorm(h, norm_mlp_g[layer])
        a = jnp.einsum('bsd,df->bsf', u, w_up[layer])
        a = jnp.square(jax.nn.relu(a))
        h = h + jnp.einsum('bsf,fd->bsd', a, w_down[layer])
    return _rmsnorm(h, norm_final_g)


def setup_inputs(seed=0):
    out = dict(first_inputs(seed))
    for name, value in second_inputs(seed + 1).items():
        if name != "x":
            out[name + "_2"] = value
    return out


def reference(
    x, positions, norm_g, w_in, gate_bias, conv_w, mlstm_norm_g, w_a, q_lat_g, kv_lat_g, w_uq,
    w_ukv, q_norm_g, k_norm_g, w_b, w_out, norm_mix_g_2, w_in_2, w_fourier_2, w_out_2,
    norm_mlp_g_2, w_up_2, w_down_2, norm_final_g_2,
):
    x = first_block(
        x, positions, norm_g, w_in, gate_bias, conv_w, mlstm_norm_g, w_a, q_lat_g, kv_lat_g,
        w_uq, w_ukv, q_norm_g, k_norm_g, w_b, w_out,
    )
    return second_block(
        x, norm_mix_g_2, w_in_2, w_fourier_2, w_out_2, norm_mlp_g_2, w_up_2, w_down_2,
        norm_final_g_2,
    )


_drawn_inputs = setup_inputs


def setup_inputs(seed=0):
    import zlib

    import numpy as np

    out = dict(_drawn_inputs(seed))
    spreads = {}
    factors = {'norm_g': 6.729,
     'mlstm_norm_g': 31.607,
     'q_lat_g': 8.0,
     'kv_lat_g': 8.0,
     'q_norm_g': 8.0,
     'k_norm_g': 8.0,
     'norm_mix_g_2': 19.491,
     'norm_mlp_g_2': 19.856,
     'norm_final_g_2': 7.493}
    for name, (base, spread) in spreads.items():
        noise = np.random.default_rng([zlib.crc32(name.encode()), seed]).standard_normal(out[name].shape)
        drawn = base * np.exp(spread * noise) if base else spread * noise
        out[name] = __import__('jax').numpy.asarray(drawn.astype(out[name].dtype))
    for name, factor in factors.items():
        out[name] = (out[name] * factor).astype(out[name].dtype)
    return out
```

```python
import concourse.bass as bass
from concourse import mybir
from contextlib import ExitStack, contextmanager
import numpy as np

P = 128
TOK, TT = 256, 2
D = 2048
KT = D // P
CW = 512
H_A, DK_A, DV_A = 8, 128, 256
H_B, D_NOPE, D_ROPE, D_HQK = 16, 128, 64, 192
H_2, HD_2 = 8, 128
LORA = 512
FG, FD = 4, 256
N_SLABS = 4
EPS = 1e-6
BIG = 1e30
PIECE = 2 * CW
RING = 4
NORM_FULL = 8
NORM_LORA = 2
UNITS = 1 + 4 * (4 + 4 + 8 + 4 + 2 + 8) + 14 + 4 * (4 + 4 + 4) + 4 * 8 + 4 * 4 + 4 * N_SLABS * 8

CONSTS = {}
PARAMS = {}


def _columns(table, names):
    at = 0
    for name, n in names:
        table[name] = slice(at, at + n)
        at += n
    return at


N_CONSTS = _columns(CONSTS, [("ident", 128), ("attn_mask", 384), ("ml_mask", 256)])
EARLY = {}
N_EARLY = _columns(EARLY, [("tri", 128), ("ones", 128), ("inv_freq", 32)])
N_PARAMS = _columns(PARAMS, [("norm_g", 16), ("ml_g", 16), ("q_lat_g", 4), ("kv_lat_g", 4), ("q_nope_g", 1),
                             ("k_nope_g", 1), ("mix_g", 16), ("mlp_g", 16), ("conv_w", 64), ("gate_b", 16),
                             ("q_rope_g", 64), ("k_rope_g", 64)])


class Tally:

    def __init__(self):
        self.n, self.reg, self.step = 0, None, 0

    def add(self, k=1):
        self.n += k

    def at(self, ahead=0):
        v = self.n + ahead
        return v if self.reg is None else self.reg * self.step + v

    def cycle(self, period):
        v = self.n // period + 1
        return v if self.reg is None else self.reg * (self.step // period) + v


@contextmanager
def loop(eng, count, steps):
    with eng.Fori(0, count) as i:
        first = {t: t.n for t in steps}
        for t, k in steps.items():
            t.reg, t.step = i, k
        yield i
    for t, k in steps.items():
        assert t.n == first[t] + k, (t.n - first[t], k)
        t.n, t.reg = first[t] + count * k, None


def build(nc, stream, x_in, consts_in, early_in, params_in, pos_in, dft_in, alibi_in, fg_in, wf_in, z_store, ga_store, gb_store,
          out):
    f32, f32r, i32 = mybir.dt.float32, mybir.dt.float32r, mybir.dt.int32
    ALU, ACT, AX = mybir.AluOpType, mybir.ActivationFunctionType, mybir.AxisListType
    MUL, ADD, SUB, MAX, MIN = ALU.mult, ALU.add, ALU.subtract, ALU.max, ALU.min

    ctx = ExitStack()
    with ctx:
        base = 16512
        K = 1024

        def place(name, shape, dt, kb):
            return nc.alloc_sbuf_tensor_at(name, shape, dt, offset=base + int(kb * K))

        raw = place("raw", [P, RING, 2 * PIECE], f32, 0)
        w_hi = place("w_hi", [P, RING, PIECE], f32r, 32)
        w_lo = place("w_lo", [P, RING, PIECE], f32r, 48)
        a_hi = place("a_hi", [P, KT, TOK], f32r, 64)
        a_lo = place("a_lo", [P, KT, TOK], f32r, 80)
        nat = place("nat", [P, TT, D], f32, 96)
        qk_t = place("qk_t", [P, 2 * H_A, TOK], f32, 112)
        v_a = place("v_a", [P, TT, H_A, DV_A + 1], f32, 128)
        lat_hi = place("lat_hi", [P, 8, TOK], f32r, 144.25)
        lat_lo = place("lat_lo", [P, 8, TOK], f32r, 152.25)
        z1 = place("z1", [P, TT, D], f32, 160.25)
        z2 = place("z2", [P, TT, D], f32, 176.25)
        scr = place("scr", [P, D], f32, 160.25)
        qn_t = place("qn_t", [P, H_B, TOK], f32, 112)
        kn_t = place("kn_t", [P, H_B, TOK], f32, 128)
        yb = place("yb", [P, TT, D], f32, 144.25)
        qr_t = place("qr_t", [P, H_B // 2, TOK], f32, 160.25)
        kr_t = place("kr_t", [P, H_B // 2, TOK], f32, 168.25)
        v_b = place("v_b", [P, TT, D], f32, 176.25)
        ga = place("ga", [P, TT, D], f32, 112)
        gb = place("gb", [P, TT, D], f32, 128)
        dft = place("dft", [P, 2, 3 * FD], f32, 112)
        wf = place("wf", [P, FG, 2, FD], f32, 118)
        g_sb = place("g_sb", [P, 2, 2, 2 * FD], f32, 126)
        re_sb = place("re_sb", [P, 2, FD], f32, 134)
        y2 = place("y2", [P, TT, H_2 * HD_2], f32, 136)
        q2_t = place("q2_t", [P, H_2, TOK], f32, 144.25)
        k2_t = place("k2_t", [P, H_2, TOK], f32, 152.25)
        v2 = place("v2", [P, TT, H_2 * HD_2], f32, 160.25)
        uf = place("uf", [P, TT, FG * FD], f32, 168.25)
        alibi = place("alibi", [P, H_2, 2 * TOK], f32, 176.25)
        m_hi = place("m_hi", [P, KT, TOK], f32r, 112)
        m_lo = place("m_lo", [P, KT, TOK], f32r, 128)
        fg = place("fg", [P, D], f32, 144.25)
        sq_end = place("sq_end", [P, D], f32, 152.25)
        e_at = 180.25
        early = place("early", [P, N_EARLY], f32, e_at)
        mrow = place("mrow", [8, 2, P + TOK], f32, e_at + 2)
        sm = place("sm", [P, TT, 80], f32, e_at + 5)
        tmp = place("tmp", [P, TT, 32], f32, e_at + 6)
        f_nat = place("f_nat", [P, TT, 8], f32, e_at + 7)
        lf = place("lf", [P, TT, 8], f32, e_at + 7.25)
        at = 192.25
        cst = place("cst", [P, N_CONSTS], f32, at)
        at += N_CONSTS * 4 / K
        par = place("par", [P, N_PARAMS], f32, at)
        at += N_PARAMS * 4 / K
        at = -(-at * K // 32) * 32 / K
        stg = place("stg", [P, TT, CW], f32, at)
        stg2 = place("stg2", [P, TT, CW], f32, at + 4)
        at += 8
        small = {}

        def little(name, shape, dt=f32):
            nonlocal at
            n = 1
            for s in shape[1:]:
                n *= s
            t = place(name, shape, dt, at)
            at += -(-n * 4 // 32) * 32 / K
            small[name] = t
            return t

        neg_half = little("neg_half", [P, 32])
        kr = little("kr", [P, TT, 64])
        cos = little("cos", [P, TT, 32])
        sin = little("sin", [P, TT, 32])
        m_fin = little("m_fin", [8, TOK])
        a_nat = little("a_nat", [P, TT, 8])
        expm = little("expm", [P, TT, 8])
        pos_i = little("pos_i", [P, TT], i32)
        pos_f = little("pos_f", [P, TT])
        ss1 = little("ss1", [P, TT])
        ms1 = little("ms1", [P, TT])
        inv1 = little("inv1", [P, TT])
        ss_l = little("ss_l", [P, 2, TT])
        ms_l = little("ms_l", [P, 2, TT])
        inv_l = little("inv_l", [P, 2, TT])
        ml_ss = little("ml_ss", [P, TT])
        ml_r = little("ml_r", [P, TT])
        ml_t = little("ml_t", [P, TT])
        ml_ms = little("ml_ms", [P, TT])
        ml_f = little("ml_f", [P, TT])
        ss_kr = little("ss_kr", [P, TT])
        ss_q = little("ss_q", [P, TT, H_B])
        ss_qr = little("ss_qr", [P, TT, H_B])
        inv_q = little("inv_q", [P, TT, H_B])
        ss_k = little("ss_k", [P, TT, 4])
        inv_k = little("inv_k", [P, TT, 4])
        nmax = little("nmax", [P, 2, TT])
        nb = little("nb", [P, 2, TT])
        den = little("den", [P, 2, TT])
        rden = little("rden", [P, TT])
        ss2 = little("ss2", [P, TT, 4])
        inv2 = little("inv2", [P, TT])
        inv3 = little("inv3", [P, TT])
        inv4 = little("inv4", [P, TT])
        assert base + at * K <= nc.sbuf_usable_end, (at, nc.sbuf_usable_end)

        def psum(name, shape=(P, 512)):
            return ctx.enter_context(nc.psum_tensor(name, list(shape), f32))

        proj = [psum(f"proj{i}") for i in range(4)]
        tbank = [psum(f"tbank{i}") for i in range(2)]
        bank_a = psum("bank_a")
        bank_b = psum("bank_b")

        ident = cst[:, CONSTS["ident"]]

        def par_c(name, i=0):
            s = PARAMS[name]
            return par[:, s.start + i:s.start + i + 1]

        def sem(name):
            return ctx.enter_context(nc.semaphore(name))

        raw_landed = [sem(f"raw_landed{i}") for i in range(RING)]
        w_rounded = sem("w_rounded")
        w_rest = sem("w_rest")
        w_used = sem("w_used")
        proj_read = sem("proj_read")
        t_done = sem("t_done")
        t_hi = sem("t_hi")
        t_by_act = sem("t_by_act")
        t_by_dve = sem("t_by_dve")
        x_ready = sem("x_ready")
        cst_ready = sem("cst_ready")
        early_ready = sem("early_ready")
        par_ready = sem("par_ready")
        pos_ready = sem("pos_ready")
        dve_seq = sem("dve_seq")
        act_seq = sem("act_seq")
        pow_asked = sem("pow_asked")
        pow_done = sem("pow_done")
        pool_init = sem("pool_init")
        staged = sem("staged")
        sumsq = sem("sumsq")
        trig_arg = sem("trig_arg")
        trig = sem("trig")
        gate_in = sem("gate_in")
        gate_ln = sem("gate_ln")
        lf_ready = sem("lf_ready")
        f_sum = sem("f_sum")
        a_ready = sem("a_ready")
        a_row = sem("a_row")
        m_row = sem("m_row")
        m_col = sem("m_col")
        m_sum = sem("m_sum")
        m_exp = sem("m_exp")
        conv_done = sem("conv_done")
        conv_sig = sem("conv_sig")
        qk_ready = sem("qk_ready")
        sig = sem("sig")
        gated = sem("gated")
        z_out = sem("z_out")
        z_full = sem("z_full")
        v_ready = sem("v_ready")
        ml_s = sem("ml_s")
        ml_e = sem("ml_e")
        ml_w = sem("ml_w")
        ml_p = sem("ml_p")
        ml_o = sem("ml_o")
        ml_q = sem("ml_q")
        ml_done = sem("ml_done")
        squared = sem("squared")
        k_scaled = sem("k_scaled")
        yb_in = sem("yb_in")
        s_done = sem("s_done")
        s_read = sem("s_read")
        b_ready = sem("b_ready")
        p_ready = sem("p_ready")
        o_done = sem("o_done")
        o_read = sem("o_read")
        g_in = [sem("ga_in"), sem("gb_in")]
        x_again = sem("x_again")
        res_ready = sem("res_ready")
        alibi_in_s = sem("alibi_in_s")
        dft_in_s = sem("dft_in_s")
        uf_ready = sem("uf_ready")
        f_g = sem("f_g")
        f_ge = sem("f_ge")
        f_r = sem("f_r")
        f_re = sem("f_re")
        f_y = sem("f_y")
        f_hi = sem("f_hi")
        f_lo = sem("f_lo")
        relu = sem("relu")
        fg_in_s = sem("fg_in_s")
        out_ready = sem("out_ready")
        stored = sem("stored")

        GATED_IN = 2 + 8 + 8

        def wait(eng, s, value):
            if not isinstance(value, int) or value > 0:
                eng.wait_ge(s, value)

        x_v = x_in.rearrange("(t p) d -> p t d", p=P)
        out_v = out.rearrange("(t p) d -> p t d", p=P)
        block = ctx.enter_context(nc.Block())

        PIECES = 2 * UNITS

        @block.sync
        def _(sp):
            sp.dma_start(cst[:, :], consts_in).then_inc(cst_ready, 16)
            sp.dma_start(early[:, :], early_in).then_inc(early_ready, 16)
            sp.dma_start(nat[:, :, :], x_v).then_inc(x_ready, 16)
            for u in range(RING):
                sp.dma_start(raw[:, u, :], stream[u]).then_inc(raw_landed[u], 16)
            whole, rest = divmod(UNITS - RING, RING)
            with sp.Fori(0, whole) as i:
                for j in range(RING):
                    sp.wait_ge(w_rest, i * (2 * RING) + 2 * j + 2)
                    sp.dma_start(raw[:, j, :], stream[bass.ds(i * RING + (RING + j), 1)].rearrange("o p n -> (o p) n")
                                 ).then_inc(raw_landed[j], 16)
            for j in range(rest):
                sp.wait_ge(w_rest, 2 * RING * whole + 2 * j + 2)
                sp.dma_start(raw[:, j, :], stream[RING * (whole + 1) + j]).then_inc(raw_landed[j], 16)
            for t in range(TT):
                sp.wait_ge(out_ready, t + 1)
                sp.dma_start(out_v[:, t, :], nat[:, t, :]).then_inc(stored, 16)
            sp.wait_ge(stored, 32)

        @block.gpsimd
        def _(pool):
            pool.dma_start(pos_i[:, :], pos_in).then_inc(pos_ready, 16)
            pool.dma_start(par[:, :], params_in).then_inc(par_ready, 16)
            nc.gpsimd.memset(neg_half[:, :], -0.5).then_inc(pool_init, 1)
            nc.gpsimd.memset(v_a[:, :, :, DV_A:DV_A + 1], 1.0).then_inc(pool_init, 1)
            nc.gpsimd.memset(mrow[:, :, 0:P], 0.0).then_inc(pool_init, 1)
            pool.wait_ge(pool_init, 1)
            asked = Tally()

            def power(dst, src, width):
                asked.add()
                pool.wait_ge(pow_asked, asked.at())
                nc.gpsimd.tensor_tensor(dst, src, neg_half[:, 0:width], ALU.pow).then_inc(pow_done, 1)

            flat = lambda ap: ap.rearrange("p a b -> p (a b)")
            power(inv1[:, :], ms1[:, :], TT)
            pool.wait_ge(z_full, 1)
            pool.dma_start(z_store, z1[:, :, :]).then_inc(z_out, 16)
            power(flat(inv_l[:, :, :]), flat(ms_l[:, :, :]), 2 * TT)
            for h in range(4):
                power(ml_f[:, :], ml_ms[:, :], TT)
            pool.wait_ge(z_full, 2)
            pool.dma_start(ga_store, z2[:, :, :]).then_inc(z_out, 16)
            for h in range(4, H_A):
                power(ml_f[:, :], ml_ms[:, :], TT)
            pool.wait_ge(z_full, 3)
            pool.dma_start(gb_store, z1[:, :, :]).then_inc(z_out, 16)
            power(flat(inv_q[:, :, :]), flat(ss_q[:, :, :]), TT * H_B)
            for i in range(4):
                power(flat(inv_k[:, :, :]), flat(ss_k[:, :, :]), TT * 4)
            pool.wait_ge(w_used, RING + 2 * (1 + 4 * 30 + 14))
            pool.dma_start(yb[:, :, :], z_store).then_inc(yb_in, 16)
            pool.wait_ge(s_done, H_B)
            pool.dma_start(ga[:, :, :], ga_store).then_inc(g_in[0], 16)
            pool.dma_start(gb[:, :, :], gb_store).then_inc(g_in[1], 16)
            pool.wait_ge(w_used, RING + 2 * (1 + 4 * 30 + 14 + 4 * 8) + 1)
            pool.dma_start(yb[:, :, :], x_v).then_inc(x_again, 16)
            pool.wait_ge(gated, GATED_IN + 8)
            pool.dma_start(alibi[:, :, :], alibi_in).then_inc(alibi_in_s, 16)
            pool.dma_start(dft[:, :, :], dft_in).then_inc(dft_in_s, 16)
            pool.dma_start(wf[:, :, :, :], wf_in).then_inc(dft_in_s, 16)
            power(inv2[:, :], ms1[:, :], TT)
            power(inv3[:, :], ms1[:, :], TT)
            pool.wait_ge(s_done, H_B + H_2)
            pool.dma_start(fg[:, :], fg_in).then_inc(fg_in_s, 16)
            power(inv4[:, :], ms1[:, :], TT)

        @block.tensor
        def _(pe):
            piece, chunk, tr = Tally(), Tally(), Tally()
            by_act, by_dve = Tally(), Tally()
            used = {by_act: t_by_act, by_dve: t_by_dve}
            readers = []

            def group(src, by, n=4):
                if len(readers) > 1:
                    pe.wait_ge(used[readers[-2]], readers[-2].at(-1 if readers[-1] is readers[-2] else 0))
                readers.append(by)
                by.add()
                for b in range(n):
                    last = nc.tensor.transpose(tbank[tr.n % 2][:, b * P:(b + 1) * P], src(b), ident)
                last.then_inc(t_done, 1)
                tr.add()

            def from_nat(buf, g):
                return lambda b: buf[:, b % 2, (2 * g + b // 2) * P:(2 * g + b // 2 + 1) * P]

            def project(hi, lo, k0=0, pieces=NORM_FULL, slot=None, before=None):
                banks = [proj[2 * (chunk.n % 2) + t] for t in range(TT)]
                wait(pe, proj_read, (chunk.at(-1) if chunk.reg is None else chunk.at(-1)) * 2)
                for j in range(pieces):
                    if before:
                        before(j)
                    pe.wait_ge(w_rest, piece.at(1))
                    s = piece.n % RING
                    for k in range(2):
                        kt = k0 + 2 * j + k
                        wh, wl = w_hi[:, s, k * CW:(k + 1) * CW], w_lo[:, s, k * CW:(k + 1) * CW]
                        for t in range(TT):
                            ah, al = hi[:, kt, t * P:(t + 1) * P], lo[:, kt, t * P:(t + 1) * P]
                            first, end = j == 0 and k == 0, j == pieces - 1 and k == 1
                            nc.tensor.matmul(banks[t][:, :], ah, wh, start=first, stop=False)
                            nc.tensor.matmul(banks[t][:, :], ah, wl, start=False, stop=False)
                            last = nc.tensor.matmul(banks[t][:, :], al, wh, start=False, stop=end)
                    last.then_inc(w_used, 1)
                    piece.add()
                    if slot:
                        slot(j)
                chunk.add()

            def jit(buf, n0=0, n=8):
                g0 = by_dve.n - n0
                for g in range(n0, n0 + 2):
                    group(from_nat(buf, g - n0), by_dve)

                def slot(j):
                    if n0 + 2 <= j + 2 < n0 + n:
                        group(from_nat(buf, j + 2 - n0), by_dve)
                    elif n0 and j + 2 < n0 + 2:
                        pass

                def before(j):
                    if n0 <= j < n0 + n:
                        pe.wait_ge(t_by_dve, g0 + j + 1)
                return slot, before

            pe.sem_inc(w_used, RING)
            pe.wait_ge(cst_ready, 16)
            pe.wait_ge(x_ready, 16)
            for g in range(8):
                group(from_nat(nat, g), by_dve)
            pe.wait_ge(t_by_dve, 8)

            for j in range(2):
                pe.wait_ge(w_rest, piece.at(1))
                s = piece.n % RING
                for k in range(8):
                    kt = 8 * j + k
                    for t in range(TT):
                        wh, wl = w_hi[:, s, k * P:(k + 1) * P], w_lo[:, s, k * P:(k + 1) * P]
                        ah, al = a_hi[:, kt, t * P:(t + 1) * P], a_lo[:, kt, t * P:(t + 1) * P]
                        o = proj[t][:, 0:P]
                        nc.tensor.matmul(o, ah, wh, start=(kt == 0), stop=False)
                        nc.tensor.matmul(o, ah, wl, start=False, stop=False)
                        last = nc.tensor.matmul(o, al, wh, start=False, stop=(kt == KT - 1))
                last.then_inc(w_used, 1)
                piece.add()
            chunk.add()

            def gates_slot(j):
                tri, ones = early[:, EARLY["tri"]], early[:, EARLY["ones"]]
                if j == 1:
                    pe.wait_ge(lf_ready, 1)
                    nc.tensor.matmul(bank_a[:, 0:8], tri, lf[:, 0, :], start=True, stop=True)
                    nc.tensor.matmul(bank_a[:, 8:16], ones, lf[:, 0, :], start=True, stop=False)
                    nc.tensor.matmul(bank_a[:, 8:16], tri, lf[:, 1, :], start=False, stop=True).then_inc(f_sum, 1)
                if j == 2:
                    pe.wait_ge(a_ready, 1)
                    for t in range(TT):
                        last = nc.tensor.transpose(bank_b[0:8, t * P:(t + 1) * P], a_nat[:, t, :], ident)
                    last.then_inc(a_row, 1)
                if j == 3:
                    pe.wait_ge(m_row, 1)
                    for t in range(TT):
                        last = nc.tensor.transpose(bank_a[:, 16 + 8 * t:24 + 8 * t], m_fin[:, t * P:(t + 1) * P],
                                                   cst[0:8, 0:8])
                    last.then_inc(m_col, 1)

            def stg_slot(j, n, by=by_dve, more=None):
                if j == 0:
                    pe.wait_ge(staged, n)
                if j < 2:
                    group(from_nat(stg, j), by)
                if more:
                    more(j)

            project(a_hi, a_lo, slot=gates_slot)
            for i in range(1, 4):
                project(a_hi, a_lo, slot=lambda j: stg_slot(j, i))
            project(a_hi, a_lo, slot=lambda j: stg_slot(j, 4))
            for i in range(3):
                project(a_hi, a_lo)
            with loop(pe, 6, {piece: 16, chunk: 2}):
                project(a_hi, a_lo)
                project(a_hi, a_lo)
            project(a_hi, a_lo)
            project(a_hi, a_lo, slot=lambda j: stg_slot(j, 5))

            def mlstm_slot(h):
                def slot(j):
                    if h == 0:
                        stg_slot(j, 6)
                    if j == 1:
                        if h == 0:
                            pe.wait_ge(qk_ready, 8)
                            pe.wait_ge(m_row, 1)
                        wait(pe, ml_done, h)
                        q, k = qk_t[:, h, :], qk_t[:, H_A + h, :]
                        nc.tensor.matmul(bank_a[:, 0:TOK], k[:, 0:P], q, start=True, stop=True)
                        nc.tensor.matmul(bank_a[:, TOK:TOK + P], k[:, P:TOK], q[:, P:TOK], start=True, stop=True)
                        nc.tensor.matmul(bank_b[:, 0:TOK], cst[0:8, h:h + 1].to_broadcast([8, P]), m_fin[:, :],
                                         start=True, stop=True).then_inc(ml_s, 1)
                    if j == 3:
                        pe.wait_ge(ml_p, h + 1)
                        if h == 0:
                            pe.wait_ge(v_ready, 8)
                            pe.wait_ge(pool_init, 3)
                        pt = stg2[:, 1, 0:384]
                        nc.tensor.matmul(bank_b[:, 0:DV_A + 1], pt[:, 0:P], v_a[:, 0, h, :], start=True, stop=True)
                        nc.tensor.matmul(bank_a[:, 0:DV_A + 1], pt[:, P:2 * P], v_a[:, 0, h, :], start=True, stop=False)
                        nc.tensor.matmul(bank_a[:, 0:DV_A + 1], pt[:, 2 * P:3 * P], v_a[:, 1, h, :], start=False,
                                         stop=True).then_inc(ml_o, 1)
                return slot

            for h in range(H_A):
                project(a_hi, a_lo, slot=mlstm_slot(h))

            def q_slot(j, n, buf):
                if j == 0:
                    pe.wait_ge(staged, n)
                group(from_nat(buf, j), by_act)

            pe.wait_ge(ml_done, H_A)
            project(lat_hi, lat_lo, pieces=NORM_LORA)
            for i in range(1, 5):
                project(lat_hi, lat_lo, pieces=NORM_LORA, slot=lambda j: q_slot(j, 6 + i, stg))
            project(lat_hi, lat_lo, pieces=NORM_LORA, slot=lambda j: q_slot(j, 11, stg2))
            project(lat_hi, lat_lo, k0=4, pieces=NORM_LORA, slot=lambda j: q_slot(j, 12, stg2))

            def k_slot(i):
                def slot(j):
                    if j == 1:
                        pe.wait_ge(k_scaled, i)
                        group(from_nat(stg, 0), by_act)
                        group(from_nat(stg, 1), by_act)
                        group(from_nat(stg2, 0), by_act)
                return slot

            for i in range(1, 5):
                project(lat_hi, lat_lo, k0=4, pieces=NORM_LORA, slot=k_slot(i))
            for i in range(3):
                project(lat_hi, lat_lo, k0=4, pieces=NORM_LORA)

            def scores_b(h):
                wait(pe, s_read, h)
                r = slice(64 * (h % 2), 64 * (h % 2) + 64)
                for t, keys, to in ((0, P, 0), (1, TOK, P)):
                    q = slice(t * P, (t + 1) * P)
                    nc.tensor.matmul(bank_a[:, to:to + keys], qn_t[:, h, q], kn_t[:, h, 0:keys], start=True, stop=False)
                    last = nc.tensor.matmul(bank_a[:, to:to + keys], qr_t[r, h // 2, q], kr_t[r, h // 2, 0:keys],
                                            start=False, stop=True)
                last.then_inc(s_done, 1)

            def probs_b(h):
                pe.wait_ge(p_ready, h + 1)
                group(lambda b: stg[:, h % 2, b * P:(b + 1) * P], by_act, n=3)
                return by_act.n

            def values_b(h, n):
                pe.wait_ge(t_by_act, n)
                wait(pe, o_read, h)
                pt = stg2[:, h % 2, 0:384]
                v0, v1 = v_b[:, 0, h * P:(h + 1) * P], v_b[:, 1, h * P:(h + 1) * P]
                nc.tensor.matmul(bank_b[:, 0:P], pt[:, 0:P], v0, start=True, stop=True)
                nc.tensor.matmul(bank_b[:, P:2 * P], pt[:, P:2 * P], v0, start=True, stop=False)
                nc.tensor.matmul(bank_b[:, P:2 * P], pt[:, 2 * P:3 * P], v1, start=False, stop=True).then_inc(o_done, 1)

            t_of = {}
            ya_slot, ya_before = jit(nat)
            for c in range(4):
                def slot(j, c=c):
                    if c == 0:
                        ya_slot(j)
                    h, second = divmod(8 * c + j, 2)
                    if second:
                        t_of[h] = probs_b(h)
                    else:
                        if h == 0:
                            pe.wait_ge(proj_read, 2 * 45)
                        scores_b(h)
                        if h:
                            values_b(h - 1, t_of[h - 1])
                project(a_hi, a_lo, slot=slot, before=ya_before if c == 0 else None)
            values_b(H_B - 1, t_of[H_B - 1])

            pe.wait_ge(o_read, H_B)
            yb_slot, yb_before = jit(yb)
            project(a_hi, a_lo, slot=yb_slot, before=yb_before)
            for c in range(3):
                project(a_hi, a_lo)
            pe.wait_ge(gated, GATED_IN + 2)
            y_slot, y_before = jit(nat)

            def y_slot_all(j):
                if j == 2:
                    pe.wait_ge(gated, GATED_IN + 8)
                y_slot(j)
            project(a_hi, a_lo, slot=y_slot_all, before=y_before)
            for c in range(3):
                project(a_hi, a_lo)
            pe.wait_ge(res_ready, 2)
            r_slot, r_before = jit(nat)

            def r_slot_all(j):
                if j == 2:
                    pe.wait_ge(res_ready, 8)
                r_slot(j)
            project(a_hi, a_lo, slot=r_slot_all, before=r_before)
            for i in range(4):
                project(a_hi, a_lo, slot=lambda j: stg_slot(j, 13 + i, by_act))
            project(a_hi, a_lo)

            def scores_2(h):
                wait(pe, s_read, H_B + h)
                if h == 0:
                    pe.wait_ge(t_by_act, by_act.n)
                for t in range(TT):
                    last = nc.tensor.matmul(bank_a[:, t * TOK:(t + 1) * TOK], q2_t[:, h, t * P:(t + 1) * P], k2_t[:, h, :],
                                            start=True, stop=True)
                last.then_inc(s_done, 1)

            def probs_2(h):
                pe.wait_ge(p_ready, H_B + h + 1)
                group(lambda b: stg[:, h % 2, b * P:(b + 1) * P], by_act)
                return by_act.n

            def values_2(h, n):
                pe.wait_ge(t_by_act, n)
                wait(pe, o_read, H_B + h)
                pt = stg2[:, h % 2, :]
                for t in range(TT):
                    for kt in range(2):
                        b = 2 * t + kt
                        last = nc.tensor.matmul(bank_b[:, t * P:(t + 1) * P], pt[:, b * P:(b + 1) * P],
                                                v2[:, kt, h * P:(h + 1) * P], start=(kt == 0), stop=(kt == 1))
                last.then_inc(o_done, 1)

            for c in range(2):
                def slot(j, c=c):
                    h, second = divmod(8 * c + j, 2)
                    if second:
                        t_of[h] = probs_2(h)
                    else:
                        if h == 0:
                            pe.wait_ge(proj_read, 2 * (45 + 12 + 6))
                        scores_2(h)
                        if h:
                            values_2(h - 1, t_of[h - 1])
                project(a_hi, a_lo, slot=slot)
            values_2(H_2 - 1, t_of[H_2 - 1])

            def positions_dft(g):
                wait(pe, f_ge, 2 * (g - 1))
                for ct in range(2):
                    for kt in range(2):
                        last = nc.tensor.matmul(proj[2 * (g % 2) + ct][:, :],
                                                uf[:, kt, g * FD + ct * P:g * FD + (ct + 1) * P],
                                                dft[:, kt, 0:2 * FD], start=(kt == 0), stop=(kt == 1))
                    last.then_inc(f_g, 1)

            def channels_dft(g):
                pe.wait_ge(f_ge, 2 * g + 2)
                wait(pe, f_re, g)
                if g == 0:
                    pe.wait_ge(s_read, H_B + H_2)
                for c2 in range(2):
                    for n, (ct, part) in enumerate(((0, 0), (1, 0), (0, 1), (1, 1))):
                        last = nc.tensor.matmul(bank_a[:, c2 * FD:(c2 + 1) * FD],
                                                dft[:, ct, 2 * part * FD + c2 * P:2 * part * FD + (c2 + 1) * P],
                                                g_sb[:, g % 2, ct, part * FD:(part + 1) * FD], start=(n == 0), stop=(n == 3))
                last.then_inc(f_r, 1)

            def fourier_map(g):
                pe.wait_ge(f_re, g + 1)
                wait(pe, f_lo, g)
                if g == 0:
                    pe.wait_ge(o_read, H_B + H_2)
                for e2 in range(2):
                    for c2 in range(2):
                        last = nc.tensor.matmul(bank_b[:, e2 * FD:(e2 + 1) * FD], wf[:, g, c2, e2 * P:(e2 + 1) * P],
                                                re_sb[:, c2, :], start=(c2 == 0), stop=(c2 == 1))
                last.then_inc(f_y, 1)

            pe.wait_ge(proj_read, chunk.at() * 2)
            pe.wait_ge(dft_in_s, 32)
            positions_dft(0)
            positions_dft(1)
            for g in range(FG):
                channels_dft(g)
                if g + 2 < FG:
                    positions_dft(g + 2)
                fourier_map(g)
            g0 = by_dve.n
            group(from_nat(y2, 0), by_dve)
            group(from_nat(y2, 1), by_dve)

            def mix_before(j):
                if j < 4:
                    pe.wait_ge(f_lo, j + 1)
                else:
                    pe.wait_ge(t_by_dve, g0 + j - 3)

            def mix_slot(j):
                if j < 2:
                    group(from_nat(y2, j + 2), by_dve)
            project(a_hi, a_lo, slot=mix_slot, before=mix_before)
            for c in range(3):
                project(a_hi, a_lo)
            pe.wait_ge(res_ready, 8 + 8)
            for g in range(8):
                group(from_nat(nat, g), by_dve)
            pe.wait_ge(t_by_dve, by_dve.at())
            up = Tally()
            with loop(pe, N_SLABS, {piece: 64, chunk: 8, tr: 8, by_dve: 8, up: 4}):
                def hidden_slot(j):
                    if j == 0:
                        pe.wait_ge(relu, up.at() * 2)
                    if j < 2:
                        group(from_nat(stg, j), by_dve)

                project(a_hi, a_lo)
                for j in range(3):
                    up.add()
                    project(a_hi, a_lo, slot=lambda j: hidden_slot(j))
                up.add()

                def hidden_before(j):
                    if j == 0:
                        pe.wait_ge(t_by_dve, by_dve.at())
                    if j == 6:
                        pe.wait_ge(t_by_dve, by_dve.at())
                project(m_hi, m_lo, slot=lambda j: hidden_slot(j), before=hidden_before)
                for j in range(3):
                    project(m_hi, m_lo)
            assert piece.n == PIECES, (piece.n, PIECES)

        @block.scalar
        def _(act):
            piece, done, chunk, tr, seq = Tally(), Tally(), Tally(), Tally(), Tally()
            sums = Tally()
            A = nc.scalar.activation

            def chain(ins):
                ins.then_inc(act_seq, 1)
                seq.add()
                act.wait_ge(act_seq, seq.at())

            def split(n=1):
                for _ in range(n):
                    if piece.reg is None and piece.n >= PIECES:
                        return
                    u = piece.n // 2
                    if piece.n % 2 == 0:
                        act.wait_ge(raw_landed[u % RING], piece.cycle(2 * RING) * 16)
                    act.wait_ge(w_used, piece.at(1))
                    A(w_hi[:, piece.n % RING, :], raw[:, u % RING, (piece.n % 2) * PIECE:(piece.n % 2 + 1) * PIECE],
                      ACT.Copy).then_inc(w_rounded, 1)
                    piece.add()

            def pieces(n=NORM_FULL, slot=None, ahead=True):
                for j in range(n):
                    if ahead:
                        split()
                    if slot:
                        slot(j)
                done.add(n)

            def banks():
                act.wait_ge(w_used, done.at(RING))
                b = [proj[2 * (chunk.n % 2) + t] for t in range(TT)]
                chunk.add()
                return b

            def transposed():
                act.wait_ge(t_done, tr.at(1))
                b = tbank[tr.n % 2]
                tr.add()
                return b

            def high(dst, kt, g=None, i=0):
                b = transposed()
                if g is None:
                    last = A(dst[:, kt:kt + 2, :].rearrange("p a b -> p (a b)"), b[:, :], ACT.Copy)
                else:
                    for f in range(2):
                        last = A(dst[:, kt + f, :], b[:, f * TOK:(f + 1) * TOK], ACT.Copy, scale=par_c(g, i + f))
                last.then_inc(t_hi, 1)

            def square_sum(junk, src, dst):
                wait(act, sumsq, sums.at())
                A(junk, src, ACT.Square, accum_out=dst).then_inc(sumsq, 1)
                sums.add()

            split(4)
            act.wait_ge(par_ready, 16)
            for g in range(8):
                high(a_hi, 2 * g, "norm_g", 2 * g)
            act.wait_ge(x_ready, 16)
            for t in range(TT):
                square_sum(scr[:, :], nat[:, t, :], ss1[:, t:t + 1])
            act.wait_ge(trig_arg, 2)
            A(sin[:, :, :], sin[:, :, :], ACT.Sin).then_inc(trig, 1)
            A(cos[:, :, :], cos[:, :, :], ACT.Sin).then_inc(trig, 1)
            pieces(2)
            chunk.add()
            act.wait_ge(gate_in, 1)
            chain(A(lf[:, :, :], lf[:, :, :], ACT.Exp))
            A(lf[:, :, :], lf[:, :, :], ACT.Ln, bias=1.0).then_inc(gate_ln, 1)

            def exp_slot(j):
                if j == 3:
                    act.wait_ge(m_sum, 1)
                    A(expm[:, :, :], expm[:, :, :], ACT.Exp, scale=-1.0).then_inc(m_exp, 1)

            acc = [stg2[:, j, :] for j in range(2)]
            sgm = [z2[:, 0, j * CW:(j + 1) * CW] for j in range(2)]

            def conv_slot(j):
                if j < 2:
                    tr.add()
                    act.wait_ge(conv_done, tr.at(-8))
                    A(sgm[j], acc[j], ACT.Sigmoid).then_inc(conv_sig, 1)

            def stage(inv, n):
                for t, b in enumerate(banks()):
                    last = A(stg[:, t, :], b[:, :], ACT.Copy, scale=inv[:, t:t + 1])
                    last.then_inc(proj_read, 1)
                act.wait_ge(proj_read, chunk.at() * 2)
                act.sem_inc(staged, 1)

            act.wait_ge(pow_done, 1)
            for i in range(4):
                pieces(slot=exp_slot if i == 0 else conv_slot)
                stage(inv1, i + 1)
            for i in range(4):
                pieces(slot=conv_slot if i == 0 else None)
                for t, b in enumerate(banks()):
                    A(v_a[:, t, 2 * i:2 * i + 2, 0:DV_A], b[:, :].rearrange("p (h d) -> p h d", h=2), ACT.Copy,
                      scale=inv1[:, t:t + 1]).then_inc(proj_read, 1)
            act.wait_ge(proj_read, chunk.at() * 2)
            act.sem_inc(v_ready, 8)
            tiles = Tally()
            with loop(act, 4, {piece: 16, done: 16, chunk: 2, tiles: 2}) as i:
                pieces()
                for t, b in enumerate(banks()):
                    act.wait_ge(gated, tiles.at(2))
                    A(stg[:, t, :], b[:, :], ACT.Sigmoid, scale=inv1[:, t:t + 1]).then_inc(proj_read, 1)
                pieces()
                for t, b in enumerate(banks()):
                    A(stg2[:, t, :], b[:, :], ACT.Sigmoid, scale=inv1[:, t:t + 1]).then_inc(sig, 1)
                tiles.add(2)
            with loop(act, 2, {piece: 16, done: 16, chunk: 2, tiles: 4}) as i:
                for c in range(2):
                    pieces()
                    for t, b in enumerate(banks()):
                        act.wait_ge(gated, tiles.at(2))
                        A(stg[:, t, :], b[:, :], ACT.Sigmoid, scale=inv1[:, t:t + 1]).then_inc(sig, 1)
                    tiles.add(2)
            act.wait_ge(gated, tiles.at(2))
            for i in range(2):
                def lat_slot(j, i=i):
                    if i and j < 2:
                        high(lat_hi, 2 * j, "q_lat_g", 2 * j)
                pieces(slot=lat_slot)
                stage(inv1, 5 + i)
                for t in range(TT):
                    square_sum(stg2[:, t, :], stg[:, t, :], ss_l[:, i, t:t + 1])

            for h in range(H_A):
                def slot(j, h=h):
                    if h == 0 and j < 2:
                        high(lat_hi, 4 + 2 * j, "kv_lat_g", 2 * j)
                    if j == 1:
                        act.wait_ge(ml_e, 2 * h + 2)
                        A(stg2[:, 0, 0:384], stg2[:, 0, 0:384], ACT.Exp, scale=-1.0).then_inc(ml_w, 1)
                    if j == 3:
                        act.wait_ge(ml_o, h + 1)
                        for t, b in enumerate((bank_b, bank_a)):
                            A(stg[:, t, 0:DV_A], b[:, 0:DV_A], ACT.Square, accum_out=ml_ss[:, t:t + 1]).then_inc(ml_q, 1)
                pieces(slot=slot)
                dst = z2 if h < 4 else z1
                if h == 0:
                    act.wait_ge(z_out, 16)
                for t, b in enumerate(banks()):
                    last = A(dst[:, t, (h % 4) * CW:(h % 4 + 1) * CW], b[:, :], ACT.Copy, scale=inv1[:, t:t + 1])
                    last.then_inc(proj_read, 1)
                if h % 4 == 3:
                    act.wait_ge(proj_read, chunk.at() * 2)
                    act.sem_inc(z_full, 1)

            inv_cq, inv_ckv = inv_l[:, 0, :], inv_l[:, 1, :]

            def out_group(dst, scale=None):
                b = transposed()
                src = b[:, :]
                if scale is None:
                    A(dst.rearrange("p a b -> p (a b)"), src, ACT.Copy).then_inc(t_by_act, 1)
                else:
                    A(dst.rearrange("p a b -> p (a b)"), src, ACT.Copy, scale=scale).then_inc(t_by_act, 1)

            act.wait_ge(pow_done, 2)
            act.wait_ge(ml_done, H_A)
            for i in range(4):
                pieces(NORM_LORA, slot=(lambda j: out_group(qn_t[:, 4 * (i - 1) + 2 * j:4 * (i - 1) + 2 * j + 2, :],
                                                            par_c("q_nope_g"))) if i else None)
                wait(act, squared, i)
                stage(inv_cq, 7 + i)
            act.wait_ge(z_out, 48)
            for i in range(2):
                pieces(NORM_LORA, slot=(lambda j: out_group(qn_t[:, 12 + 2 * j:14 + 2 * j, :], par_c("q_nope_g")))
                       if i == 0 else (lambda j: out_group(qr_t[:, 2 * j:2 * j + 2, :])))
                act.wait_ge(squared if i == 0 else staged, 4 if i == 0 else 11)
                for t, b in enumerate(banks()):
                    A(stg[:, t, :], b[:, :], ACT.Copy, scale=inv_cq[:, t:t + 1]).then_inc(proj_read, 1)
            for i in range(4):
                def slot(j, i=i):
                    if i == 0:
                        out_group(qr_t[:, 4 + 2 * j:6 + 2 * j, :])
                    elif j == 1:
                        k_groups(i - 1)

                def k_groups(i):
                    for f in range(2):
                        out_group(kn_t[:, 4 * i + 2 * f:4 * i + 2 * f + 2, :], par_c("k_nope_g"))
                    out_group(kr_t[:, 2 * i:2 * i + 2, :])
                pieces(NORM_LORA, slot=slot)
                if i == 0:
                    act.wait_ge(staged, 12)
                for t, b in enumerate(banks()):
                    A(stg[:, t, :], b[:, :], ACT.Copy, scale=inv_ckv[:, t:t + 1]).then_inc(proj_read, 1)
            for i in range(4):
                pieces(NORM_LORA, slot=(lambda j: k_groups(3) if j == 1 else None) if i == 0 else None)
                for t, b in enumerate(banks()):
                    A(v_b[:, t, i * CW:(i + 1) * CW], b[:, :], ACT.Copy, scale=inv_ckv[:, t:t + 1]).then_inc(proj_read, 1)
            assert chunk.n == 45, chunk.n

            for g in range(2):
                high(a_hi, 2 * g, "ml_g", 2 * g)
            for c in range(4):
                def slot(j, c=c):
                    if c == 0 and j < 6:
                        high(a_hi, 2 * (j + 2), "ml_g", 2 * (j + 2))
                    h, second = divmod(8 * c + j, 2)
                    if second:
                        b = transposed()
                        wait(act, o_done, h - 1)
                        A(stg2[:, h % 2, 0:384], b[:, 0:384], ACT.Copy).then_inc(t_by_act, 1)
                    else:
                        act.wait_ge(b_ready, h + 1)
                        s = stg[:, h % 2, :]
                        A(s[:, 0:P], s[:, 0:P], ACT.Exp, bias=nb[:, h % 2, 0:1], scale=inv_q[:, 0, h:h + 1],
                          accum_out=den[:, h % 2, 0:1])
                        A(s[:, P:384], s[:, P:384], ACT.Exp, bias=nb[:, h % 2, 1:2], scale=inv_q[:, 1, h:h + 1],
                          accum_out=den[:, h % 2, 1:2]).then_inc(p_ready, 1)
                pieces(slot=slot)
                for t, b in enumerate(banks()):
                    A(nat[:, t, c * CW:(c + 1) * CW], b[:, :], ACT.Copy).then_inc(proj_read, 1)
            for g in range(2):
                high(a_hi, 2 * g)
            act.wait_ge(g_in[0], 16)
            act.wait_ge(g_in[1], 16)
            for c in range(4):
                def slot(j, c=c):
                    if c == 0 and j < 6:
                        high(a_hi, 2 * (j + 2))
                    if j == 6:
                        act.wait_ge(gated, GATED_IN + 2 * c)
                        for t in range(TT):
                            A(stg[:, t, :], ga[:, t, c * CW:(c + 1) * CW], ACT.Sigmoid).then_inc(sig, 1)
                            A(stg2[:, t, :], gb[:, t, c * CW:(c + 1) * CW], ACT.Sigmoid).then_inc(sig, 1)
                pieces(slot=slot)
                chunk.add()
            for g in range(2):
                high(a_hi, 2 * g)

            def res_squares(c, n):
                act.wait_ge(res_ready, n)
                for t in range(TT):
                    square_sum(stg2[:, t, :], nat[:, t, c * CW:(c + 1) * CW], ss2[:, t, c:c + 1])

            for c in range(4):
                def slot(j, c=c):
                    if c == 0 and j < 6:
                        high(a_hi, 2 * (j + 2))
                    if c and j == 0:
                        res_squares(c - 1, 2 * c)
                pieces(slot=slot)
                chunk.add()
            for g in range(2):
                high(a_hi, 2 * g, "mix_g", 2 * g)
            res_squares(3, 8)
            for i in range(4):
                def slot(j, i=i):
                    if i == 0:
                        if j < 6:
                            high(a_hi, 2 * (j + 2), "mix_g", 2 * (j + 2))
                    elif j < 2:
                        dst = (q2_t, k2_t)[(i - 1) // 2]
                        out_group(dst[:, 4 * ((i - 1) % 2) + 2 * j:4 * ((i - 1) % 2) + 2 * j + 2, :])
                pieces(slot=slot)
                if i == 0:
                    act.wait_ge(pow_done, 16)
                stage(inv2, 13 + i)
            for i in range(2):
                pieces(slot=(lambda j: out_group(k2_t[:, 4 + 2 * j:6 + 2 * j, :]) if j < 2 else None) if i == 0 else None)
                for t, b in enumerate(banks()):
                    A(v2[:, t, i * CW:(i + 1) * CW], b[:, :], ACT.Copy, scale=inv2[:, t:t + 1]).then_inc(proj_read, 1)
            for c in range(2):
                def slot(j, c=c):
                    h, second = divmod(8 * c + j, 2)
                    if second:
                        b = transposed()
                        wait(act, o_done, H_B + h - 1)
                        A(stg2[:, h % 2, :], b[:, :], ACT.Copy).then_inc(t_by_act, 1)
                    else:
                        act.wait_ge(b_ready, H_B + h + 1)
                        s = stg[:, h % 2, :]
                        for t in range(TT):
                            last = A(s[:, t * TOK:(t + 1) * TOK], s[:, t * TOK:(t + 1) * TOK], ACT.Exp,
                                     bias=nmax[:, h % 2, t:t + 1], accum_out=den[:, h % 2, t:t + 1])
                        last.then_inc(p_ready, 1)
                pieces(slot=slot)
                for t, b in enumerate(banks()):
                    A(uf[:, t, c * CW:(c + 1) * CW], b[:, :], ACT.Copy, scale=inv2[:, t:t + 1]).then_inc(proj_read, 1)
            def dft_out(g):
                wait(act, f_r, g - 1)
                for ct in range(2):
                    act.wait_ge(f_g, 2 * g + ct + 1)
                    A(g_sb[:, g % 2, ct, :], proj[2 * (g % 2) + ct][:, :], ACT.Copy, scale=1.0 / FD).then_inc(f_ge, 1)

            dft_out(0)
            dft_out(1)
            for g in range(FG):
                if g + 2 < FG:
                    dft_out(g + 2)
                act.wait_ge(f_y, g + 1)
                A(a_hi[:, 2 * g:2 * g + 2, :].rearrange("p a b -> p (a b)"), bank_b[:, :], ACT.Copy).then_inc(f_hi, 1)
            high(a_hi, 8)
            high(a_hi, 10)
            for c in range(4):
                def slot(j, c=c):
                    if c == 0 and j < 2:
                        high(a_hi, 12 + 2 * j)
                    if c and j == 3:
                        res_squares(c - 1, 8 + 2 * c)
                pieces(slot=slot)
                chunk.add()
            for g in range(8):
                if g == 6:
                    pass
                high(a_hi, 2 * g, "mlp_g", 2 * g)
            res_squares(3, 16)
            act.wait_ge(pow_done, 17)
            steps = Tally()
            n_last = 64

            def slab(last):
                for c in range(8):
                    def slot(j, c=c):
                        if 1 <= c <= 4 and j < 2:
                            high(m_hi, 4 * (c - 1) + 2 * j)
                    pieces(slot=slot)
                    if c < 4:
                        for t, b in enumerate(banks()):
                            A(stg[:, t, :], b[:, :], ACT.Relu, scale=inv3[:, t:t + 1]).then_inc(proj_read, 1)
                    else:
                        chunk.add()
            with loop(act, N_SLABS - 1, {piece: 64, done: 64, chunk: 8, tr: 8}):
                slab(False)
            slab(True)
            act.wait_ge(res_ready, 8 + 8 + 8 * N_SLABS)
            for t in range(TT):
                square_sum(sq_end[:, :], nat[:, t, :], ss1[:, t:t + 1])

        @block.vector
        def _(dve):
            piece, done, chunk, tr, seq, his = (Tally() for _ in range(6))
            V = nc.vector

            def chain(ins):
                ins.then_inc(dve_seq, 1)
                seq.add()
                dve.wait_ge(dve_seq, seq.at())

            def split(n=1):
                for _ in range(n):
                    if piece.reg is None and piece.n >= PIECES:
                        return
                    dve.wait_ge(w_rounded, piece.at(1))
                    u, s = piece.n // 2, piece.n % RING
                    V.tensor_tensor(w_lo[:, s, :], raw[:, u % RING, (piece.n % 2) * PIECE:(piece.n % 2 + 1) * PIECE],
                                    w_hi[:, s, :].bitcast(f32), SUB).then_inc(w_rest, 1)
                    piece.add()

            def pieces(n=NORM_FULL, slot=None):
                for j in range(n):
                    split()
                    if slot:
                        slot(j)
                done.add(n)

            def banks():
                dve.wait_ge(w_used, done.at(RING))
                b = [proj[2 * (chunk.n % 2) + t] for t in range(TT)]
                chunk.add()
                return b

            def low(hi, lo, kt, g=None, i=0):
                his.add()
                dve.wait_ge(t_hi, his.at())
                b = tbank[tr.n % 2]
                tr.add()
                if g is None:
                    last = V.tensor_tensor(lo[:, kt:kt + 2, :].rearrange("p a b -> p (a b)"), b[:, :],
                                           hi[:, kt:kt + 2, :].rearrange("p a b -> p (a b)").bitcast(f32), SUB)
                else:
                    for f in range(2):
                        last = V.scalar_tensor_tensor(lo[:, kt + f, :], b[:, f * TOK:(f + 1) * TOK], par_c(g, i + f),
                                                      hi[:, kt + f, :].bitcast(f32), MUL, SUB)
                last.then_inc(t_by_dve, 1)

            def mean(dst, src, n):
                V.tensor_scalar(dst, src, 1.0 / n, EPS, MUL, ADD).then_inc(pow_asked, 1)

            dve.sem_inc(gated, 2)
            two_pi = 2 * np.pi
            c1 = 6.28125
            c2 = float(np.float32(np.round((two_pi - c1) * 2 ** 21) / 2 ** 21))
            c3 = float(np.float32(two_pi - c1 - c2))
            magic = 1.5 * 2 ** 23
            pi_f = float(np.nextafter(np.float32(np.pi), np.float32(0)))
            dve.wait_ge(pos_ready, 16)
            dve.wait_ge(cst_ready, 16)
            dve.wait_ge(early_ready, 16)
            chain(V.tensor_copy(pos_f[:, :], pos_i[:, :]))
            for t in range(TT):
                ang, k, r = sin[:, t, :], tmp[:, t, :], cos[:, t, :]
                chain(V.tensor_scalar(ang, early[:, EARLY["inv_freq"]], pos_f[:, t:t + 1], None, MUL))
                chain(V.tensor_scalar(k, ang, 1.0 / two_pi, magic, MUL, ADD))
                chain(V.tensor_scalar(k, k, -magic, None, ADD))
                for c in (c1, c2, c3):
                    chain(V.scalar_tensor_tensor(ang, k, -c, ang, MUL, ADD))
                chain(V.tensor_scalar(r, ang, np.pi / 2, None, ADD))
                chain(V.tensor_scalar(k, r, np.pi, -two_pi, ALU.is_gt, MUL))
                chain(V.tensor_tensor(r, r, k, ADD))
                chain(V.tensor_scalar(ang, ang, pi_f, -pi_f, MIN, MAX))
                chain(V.tensor_scalar(r, r, pi_f, -pi_f, MIN, MAX))
            dve.sem_inc(trig_arg, 2)
            split(4)
            dve.wait_ge(par_ready, 16)
            for g in range(8):
                low(a_hi, a_lo, 2 * g, "norm_g", 2 * g)
            dve.wait_ge(sumsq, 2)
            mean(ms1[:, :], ss1[:, :], D)

            pieces(2)
            dve.wait_ge(pow_done, 1)
            for t, b in enumerate(banks()):
                V.tensor_scalar(sm[:, t, :], b[:, 0:80], inv1[:, t:t + 1], None, MUL).then_inc(proj_read, 1)
            dve.wait_ge(proj_read, 2)
            bias = par[:, PARAMS["gate_b"]]
            for t in range(TT):
                chain(V.tensor_tensor(sm[:, t, 64:80], sm[:, t, 64:80], bias, ADD))
            V.scalar_tensor_tensor(lf[:, :, :], sm[:, :, 72:80], -1.0, sm[:, :, 72:80], MUL, MIN).then_inc(gate_in, 1)
            kr_v = sm[:, :, 0:64]
            chain(V.tensor_tensor(kr[:, :, :], kr_v, kr_v, MUL))
            chain(V.tensor_reduce(ss_kr[:, :], kr[:, :, :], AX.X, ADD))

            def rope(dst, src, tmp_s, cs, sn):
                x1, x2 = src[..., 0:32], src[..., 32:64]
                d1, d2 = dst[..., 0:32], dst[..., 32:64]
                V.tensor_tensor(d1, x1, cs, MUL).then_inc(dve_seq, 1)
                seq.add()
                chain(V.tensor_tensor(d2, x2, sn, MUL))
                chain(V.tensor_tensor(d1, d1, d2, SUB))
                V.tensor_tensor(d2, x2, cs, MUL).then_inc(dve_seq, 1)
                seq.add()
                chain(V.tensor_tensor(x1, x1, sn, MUL))
                chain(V.tensor_tensor(d2, d2, x1, ADD))

            dve.wait_ge(trig, 2)
            gk = par[:, PARAMS["k_rope_g"]]
            for t in range(TT):
                chain(V.tensor_tensor(sm[:, t, 0:64], sm[:, t, 0:64], gk, MUL))
            rope(kr[:, :, :], sm[:, :, 0:64], None, cos[:, :, :], sin[:, :, :])

            def gates_slot(j):
                if j == 0:
                    dve.wait_ge(gate_ln, 1)
                    V.scalar_tensor_tensor(lf[:, :, :], sm[:, :, 72:80], 0.0, lf[:, :, :], MIN, SUB).then_inc(lf_ready, 1)
                if j == 1:
                    dve.wait_ge(f_sum, 1)
                    chain(V.tensor_copy(f_nat[:, :, :], bank_a[:, 0:16].rearrange("p (t h) -> p t h", t=2)))
                    V.tensor_tensor(a_nat[:, :, :], sm[:, :, 64:72], f_nat[:, :, :], SUB).then_inc(a_ready, 1)
                if j == 2:
                    dve.wait_ge(a_row, 1)
                    dve.wait_ge(pool_init, 3)
                    chain(V.tensor_copy(mrow[:, 0, P:P + TOK], bank_b[0:8, 0:TOK]))
                    for n in range(8):
                        a, b = mrow[:, n % 2, :], mrow[:, (n + 1) % 2, :]
                        chain(V.tensor_tensor(b[:, P:P + TOK], a[:, P:P + TOK], a[:, P - 2 ** n:P + TOK - 2 ** n], MAX))
                    V.tensor_scalar(m_fin[:, :], mrow[:, 0, P:P + TOK], 0.0, None, MAX).then_inc(m_row, 1)
                if j == 3:
                    dve.wait_ge(m_col, 1)
                    V.tensor_tensor(expm[:, :, :], f_nat[:, :, :], bank_a[:, 16:32].rearrange("p (t h) -> p t h", t=2),
                                    ADD).then_inc(m_sum, 1)

            acc = [stg2[:, j, :] for j in range(2)]
            sgm = [z2[:, 0, j * CW:(j + 1) * CW] for j in range(2)]
            cw = PARAMS["conv_w"].start

            def conv_slot(j, i):
                if j < 2:
                    dve.wait_ge(t_done, tr.at(1))
                    b = tbank[tr.n % 2]
                    tr.add()
                    for n in range(4):
                        for f in range(2):
                            ft = 4 * i + 2 * j + f
                            w = par[:, cw + 4 * ft + 3 - n:cw + 4 * ft + 4 - n]
                            dst, src = acc[j][:, f * TOK:(f + 1) * TOK], b[:, f * TOK:(f + 1) * TOK]
                            if n == 0:
                                last = V.tensor_scalar(dst, src, w, None, MUL)
                            else:
                                last = V.scalar_tensor_tensor(dst[:, n:TOK], src[:, 0:TOK - n], w, dst[:, n:TOK], MUL, ADD)
                            if n < 3:
                                last.then_inc(dve_seq, 1)
                                seq.add()
                        if n < 3:
                            dve.wait_ge(dve_seq, seq.at())
                    last.then_inc(conv_done, 1)
                    dve.wait_ge(conv_done, 2 * i + j + 1)
                    dve.sem_inc(t_by_dve, 1)
                elif j < 4:
                    g = j - 2
                    dve.wait_ge(conv_sig, 2 * i + g + 1)
                    V.tensor_tensor(qk_t[:, 4 * i + 2 * g:4 * i + 2 * g + 2, :].rearrange("p a b -> p (a b)"), acc[g], sgm[g],
                                    MUL).then_inc(qk_ready, 1)

            pieces(slot=gates_slot)
            done_chunks = [chunk.add()]
            for i in range(4):
                pieces(slot=lambda j: conv_slot(j, i))
                chunk.add()
            for i in range(3):
                pieces()
                chunk.add()
            tiles = Tally()
            with loop(dve, 4, {piece: 16, done: 16, chunk: 2, tiles: 2, seq: 2}) as i:
                pieces()
                chunk.add()
                pieces()
                for t, b in enumerate(banks()):
                    tiles.add()
                    dve.wait_ge(sig, tiles.at())
                    chain(V.tensor_tensor(stg2[:, t, :], stg2[:, t, :], stg[:, t, :], MUL))
                    V.scalar_tensor_tensor(nat[:, t, bass.ds(i * CW, CW)], b[:, :], inv1[:, t:t + 1], stg2[:, t, :], MUL,
                                           MUL).then_inc(gated, 1)
                    dve.wait_ge(gated, tiles.at(2))
                    dve.sem_inc(proj_read, 1)
            with loop(dve, 2, {piece: 16, done: 16, chunk: 2, tiles: 4}) as i:
                for c in range(2):
                    pieces()
                    for t, b in enumerate(banks()):
                        tiles.add()
                        dve.wait_ge(sig, tiles.at())
                        V.scalar_tensor_tensor(z1[:, t, bass.ds(i * (2 * CW) + c * CW, CW)], b[:, :], inv1[:, t:t + 1],
                                               stg[:, t, :], MUL, MUL).then_inc(gated, 1)
                        dve.wait_ge(gated, tiles.at(2))
                        dve.sem_inc(proj_read, 1)
            dve.sem_inc(z_full, 1)
            for i in range(2):
                def lat_slot(j, i=i):
                    if i and j < 2:
                        low(lat_hi, lat_lo, 2 * j, "q_lat_g", 2 * j)
                pieces(slot=lat_slot)
                chunk.add()

            mask = cst[:, CONSTS["ml_mask"]]
            for h in range(H_A):
                def slot(j, h=h):
                    if h == 0 and j < 2:
                        low(lat_hi, lat_lo, 4 + 2 * j, "kv_lat_g", 2 * j)
                    if h == 0 and j == 0:
                        dve.wait_ge(sumsq, 6)
                        mean(ms_l[:, :, :], ss_l[:, :, :], LORA)
                    e, pt = stg2[:, 0, 0:384], stg2[:, 1, 0:384]
                    if j == 1:
                        dve.wait_ge(ml_s, h + 1)
                        V.scalar_tensor_tensor(e[:, 0:TOK], bank_b[:, 0:TOK], a_nat[:, 0, h:h + 1], mask, SUB,
                                               MAX).then_inc(ml_e, 1)
                        V.scalar_tensor_tensor(e[:, TOK:384], bank_b[:, P:TOK], a_nat[:, 1, h:h + 1], mask[:, 0:P], SUB,
                                               MAX).then_inc(ml_e, 1)
                    if j == 2:
                        dve.wait_ge(ml_w, h + 1)
                        V.scalar_tensor_tensor(pt, bank_a[:, 0:384], DK_A ** -0.5, e, MUL, MUL).then_inc(ml_p, 1)
                    if j == 3:
                        dve.wait_ge(ml_q, 2 * h + 2)
                        if h == 0:
                            dve.wait_ge(m_exp, 1)
                        for t, b in enumerate((bank_b, bank_a)):
                            V.tensor_scalar(ml_t[:, t:t + 1], b[:, DV_A:DV_A + 1], -1.0, None, MUL).then_inc(dve_seq, 1)
                            seq.add()
                        dve.wait_ge(dve_seq, seq.at())
                        for t, b in enumerate((bank_b, bank_a)):
                            chain(V.scalar_tensor_tensor(ml_r[:, t:t + 1], b[:, DV_A:DV_A + 1], expm[:, t, h:h + 1],
                                                         ml_t[:, t:t + 1], MAX, MAX))
                        chain(V.reciprocal(ml_r[:, :], ml_r[:, :]))
                        chain(V.tensor_tensor(ml_t[:, :], ml_r[:, :], ml_r[:, :], MUL))
                        chain(V.tensor_tensor(ml_t[:, :], ml_t[:, :], ml_ss[:, :], MUL))
                        mean(ml_ms[:, :], ml_t[:, :], DV_A)
                    if j == 4:
                        dve.wait_ge(pow_done, 3 + h)
                        chain(V.tensor_tensor(ml_r[:, :], ml_f[:, :], ml_r[:, :], MUL))
                        for t, b in enumerate((bank_b, bank_a)):
                            o = nat[:, t, h * DV_A:(h + 1) * DV_A]
                            last = V.scalar_tensor_tensor(o, b[:, 0:DV_A], ml_r[:, t:t + 1], o, MUL, MUL)
                        last.then_inc(ml_done, 1)
                pieces(slot=slot)
                chunk.add()

            def squares(buf, width, dst):
                for t in range(TT):
                    V.tensor_tensor(stg2[:, t, :], buf[:, t, :], buf[:, t, :], MUL).then_inc(dve_seq, 1)
                    seq.add()
                for t in range(TT):
                    dve.wait_ge(dve_seq, seq.at(t - 1) if t == 0 else seq.at(-1))
                    if t:
                        dve.sem_inc(squared, 1)
                    last = V.tensor_reduce(dst(t), stg2[:, t, :].rearrange("p (h d) -> p h d", d=width), AX.X, ADD)
                    last.then_inc(dve_seq, 1)
                    seq.add()

                dve.wait_ge(dve_seq, seq.at())

            for i in range(4):
                def slot(j, i=i):
                    if i:
                        tr.add()
                pieces(NORM_LORA, slot=slot)
                chunk.add()
                dve.wait_ge(proj_read, chunk.at() * 2)
                squares(stg, D_NOPE, lambda t: ss_q[:, t, 4 * i:4 * i + 4])
            for i in range(2):
                pieces(NORM_LORA)
                tr.add(2)
                chunk.add()
                dve.wait_ge(proj_read, chunk.at() * 2)
                dve.wait_ge(t_done, tr.at())
                squares(stg, D_ROPE, lambda t: ss_qr[:, t, 8 * i:8 * i + 8])
                for t in range(TT):
                    xs = stg[:, t, :].rearrange("p (h d) -> p h d", d=64)
                    d = stg2[:, t, :].rearrange("p (h d) -> p h d", d=64)
                    g = par[:, PARAMS["q_rope_g"]].unsqueeze(1).to_broadcast([P, 8, 64])
                    chain(V.tensor_tensor(xs, xs, g, MUL))
                    rope(d, xs, None, cos[:, t, :].unsqueeze(1).to_broadcast([P, 8, 32]),
                         sin[:, t, :].unsqueeze(1).to_broadcast([P, 8, 32]))
                dve.sem_inc(staged, 1)
            V.scalar_tensor_tensor(ss_q[:, :, :], ss_q[:, :, :], D_HQK * EPS, ss_qr[:, :, :], ADD, ADD).then_inc(pow_asked, 1)

            def k_slot(j, i):
                if j == 0:
                    dve.wait_ge(pow_done, 12 + i)
                    for t in range(TT):
                        ks = stg[:, t, :].rearrange("p (h d) -> p h d", d=D_NOPE)
                        ik = inv_k[:, t, :].unsqueeze(2)
                        V.tensor_tensor(ks, ks, ik.to_broadcast([P, 4, D_NOPE]), MUL)
                        last = V.tensor_tensor(stg2[:, t, 0:256].rearrange("p (h d) -> p h d", d=64),
                                               kr[:, t, :].unsqueeze(1).to_broadcast([P, 4, 64]),
                                               ik.to_broadcast([P, 4, 64]), MUL)
                    last.then_inc(k_scaled, 1)
                if j == 1:
                    tr.add(3)

            for i in range(4):
                pieces(NORM_LORA, slot=(lambda j: k_slot(j, i - 1)) if i else (lambda j: tr.add()))
                chunk.add()
                dve.wait_ge(proj_read, chunk.at() * 2)
                dve.wait_ge(t_done, tr.at())
                squares(stg, D_NOPE, lambda t: ss_k[:, t, :])
                for t in range(TT):
                    chain(V.tensor_scalar(ss_k[:, t, :], ss_k[:, t, :], ss_kr[:, t:t + 1], None, ADD))
                mean(ss_k[:, :, :], ss_k[:, :, :], D_HQK)
            for i in range(4):
                pieces(NORM_LORA, slot=(lambda j: k_slot(j, 3)) if i == 0 else None)
                chunk.add()

            def finish_head(h, n, dst, gate):
                dve.wait_ge(o_done, n + 1)
                chain(V.reciprocal(rden[:, :], den[:, h % 2, :]))
                for t in range(TT):
                    o, b = dst[:, t, h * P:(h + 1) * P], bank_b[:, t * P:(t + 1) * P]
                    if gate:
                        last = V.scalar_tensor_tensor(o, b, rden[:, t:t + 1], o, MUL, MUL)
                    else:
                        last = V.tensor_scalar(o, b, rden[:, t:t + 1], None, MUL)
                last.then_inc(o_read, 1)

            for g in range(2):
                low(a_hi, a_lo, 2 * g, "ml_g", 2 * g)
            for c in range(4):
                def slot(j, c=c):
                    if c == 0 and j < 6:
                        low(a_hi, a_lo, 2 * (j + 2), "ml_g", 2 * (j + 2))
                    h, second = divmod(8 * c + j, 2)
                    if second:
                        tr.add()
                        return
                    s = stg[:, h % 2, 0:384]
                    dve.wait_ge(s_done, h + 1)
                    if h > 1:
                        dve.wait_ge(o_done, h - 1)
                    V.tensor_tensor(s, bank_a[:, 0:384], cst[:, CONSTS["attn_mask"]], ADD).then_inc(s_read, 1)
                    dve.wait_ge(s_read, h + 1)
                    V.tensor_reduce(nmax[:, h % 2, 0:1], s[:, 0:P], AX.X, MAX, negate=True).then_inc(dve_seq, 1)
                    seq.add()
                    chain(V.tensor_reduce(nmax[:, h % 2, 1:2], s[:, P:384], AX.X, MAX, negate=True))
                    if h == 0:
                        dve.wait_ge(pow_done, 11)
                    V.tensor_tensor(nb[:, h % 2, :], nmax[:, h % 2, :], inv_q[:, :, h], MUL).then_inc(b_ready, 1)
                    if h:
                        if h == 1:
                            dve.wait_ge(yb_in, 16)
                        finish_head(h - 1, h - 1, yb, True)
                pieces(slot=slot)
                chunk.add()
            finish_head(H_B - 1, H_B - 1, yb, True)
            for g in range(2):
                low(a_hi, a_lo, 2 * g)
            for c in range(4):
                def slot(j, c=c):
                    if c == 0 and j < 6:
                        low(a_hi, a_lo, 2 * (j + 2))
                    if j == 7:
                        for t in range(TT):
                            y = nat[:, t, c * CW:(c + 1) * CW]
                            dve.wait_ge(sig, 8 + 8 + 4 * c + 2 * t + 2)
                            V.tensor_tensor(y, y, stg[:, t, :], MUL).then_inc(dve_seq, 1)
                            seq.add()
                pieces(slot=slot)
                for t, b in enumerate(banks()):
                    y = nat[:, t, c * CW:(c + 1) * CW]
                    V.tensor_tensor(stg2[:, t, :], b[:, :], stg2[:, t, :], MUL).then_inc(proj_read, 1)
                    dve.wait_ge(proj_read, chunk.at(-1) * 2 + t + 1)
                    dve.wait_ge(dve_seq, seq.at())
                    V.tensor_tensor(y, y, stg2[:, t, :], ADD).then_inc(gated, 1)

            def add_chunk(c, other):
                for t, b in enumerate(banks()):
                    o = nat[:, t, c * CW:(c + 1) * CW]
                    V.tensor_tensor(o, b[:, :], other[:, t, c * CW:(c + 1) * CW], ADD).then_inc(res_ready, 1)
                    res.add()
                    dve.wait_ge(res_ready, res.at())
                    dve.sem_inc(proj_read, 1)

            res = Tally()
            for g in range(2):
                low(a_hi, a_lo, 2 * g)
            for c in range(4):
                pieces(slot=(lambda j: low(a_hi, a_lo, 2 * (j + 2)) if j < 6 else None) if c == 0 else None)
                if c == 0:
                    dve.wait_ge(x_again, 16)
                add_chunk(c, yb)

            def mean_of_chunks(n):
                dve.wait_ge(sumsq, n)
                chain(V.tensor_reduce(ss1[:, :], ss2[:, :, :], AX.X, ADD))
                mean(ms1[:, :], ss1[:, :], D)

            for g in range(2):
                low(a_hi, a_lo, 2 * g, "mix_g", 2 * g)
            mean_of_chunks(6 + 8)

            def in2_slot(j):
                if j < 6:
                    low(a_hi, a_lo, 2 * (j + 2), "mix_g", 2 * (j + 2))
            pieces(slot=in2_slot)
            chunk.add()
            for i in range(1, 6):
                pieces()
                chunk.add()
                if i < 5:
                    tr.add(2)
            for c in range(2):
                def slot(j, c=c):
                    h, second = divmod(8 * c + j, 2)
                    if second:
                        tr.add()
                        return
                    n = H_B + h
                    s = stg[:, h % 2, :]
                    if h == 0:
                        dve.wait_ge(alibi_in_s, 16)
                    dve.wait_ge(s_done, n + 1)
                    if h > 1:
                        dve.wait_ge(o_done, n - 1)
                    V.scalar_tensor_tensor(s, bank_a[:, :], HD_2 ** -0.5, alibi[:, h, :], MUL, ADD).then_inc(s_read, 1)
                    dve.wait_ge(s_read, n + 1)
                    V.tensor_reduce(nmax[:, h % 2, :], s.rearrange("p (t k) -> p t k", t=2), AX.X, MAX,
                                    negate=True).then_inc(b_ready, 1)
                    if h:
                        finish_head(h - 1, n - 1, y2, False)
                pieces(slot=slot)
                chunk.add()
            finish_head(H_2 - 1, H_B + H_2 - 1, y2, False)
            for g in range(FG):
                dve.wait_ge(f_r, g + 1)
                wait(dve, f_y, g)
                V.tensor_copy(re_sb[:, :, :].rearrange("p a b -> p (a b)"), bank_a[:, :]).then_inc(f_re, 1)
                dve.wait_ge(f_hi, g + 1)
                V.tensor_tensor(a_lo[:, 2 * g:2 * g + 2, :].rearrange("p a b -> p (a b)"), bank_b[:, :],
                                a_hi[:, 2 * g:2 * g + 2, :].rearrange("p a b -> p (a b)").bitcast(f32), SUB).then_inc(f_lo, 1)
            low(a_hi, a_lo, 8)
            low(a_hi, a_lo, 10)
            for c in range(4):
                pieces(slot=(lambda j: low(a_hi, a_lo, 12 + 2 * j) if j < 2 else None) if c == 0 else None)
                add_chunk(c, nat)
            for g in range(8):
                low(a_hi, a_lo, 2 * g, "mlp_g", 2 * g)
            mean_of_chunks(14 + 8)
            hid = Tally()

            def slab():
                for c in range(8):
                    def slot(j, c=c):
                        if 1 <= c <= 4 and j < 2:
                            low(m_hi, m_lo, 4 * (c - 1) + 2 * j)
                    pieces(slot=slot)
                    if c < 4:
                        chunk.add()
                        for t in range(TT):
                            dve.wait_ge(proj_read, chunk.at(-1) * 2 + t + 1)
                            V.tensor_tensor(stg[:, t, :], stg[:, t, :], stg[:, t, :], MUL).then_inc(relu, 1)
                    else:
                        add_chunk(c - 4, nat)
            with loop(dve, N_SLABS - 1, {piece: 64, done: 64, chunk: 8, tr: 8, his: 8, res: 8}):
                slab()
            slab()
            dve.wait_ge(sumsq, 22 + 2)
            mean(ms1[:, :], ss1[:, :], D)
            dve.wait_ge(fg_in_s, 16)
            dve.wait_ge(pow_done, 18)
            for t in range(TT):
                V.scalar_tensor_tensor(nat[:, t, :], nat[:, t, :], inv4[:, t:t + 1], fg[:, :], MUL, MUL).then_inc(out_ready, 1)


def _units(w):
    k, n = w.shape
    v = w.reshape(k // 512, 4, P, n // CW, CW).transpose(3, 0, 2, 1, 4)
    return v.reshape(-1, P, 4 * CW)


def _stream(i):
    s = np.cumsum([0, 1024, 1024, 2048, 2048, 8, 8, 2048, 512, 512, 64, 2048, 2048, 2048])
    w = i["w_in"][0]
    q, k, v, o, gi, gf, z, cq, ckv, kr, zb, ga, gb = (w[:, s[n]:s[n + 1]] for n in range(13))
    parts = []
    small = np.concatenate([kr, gi, gf, np.zeros((D, P - 80), w.dtype)], axis=1)
    parts.append(small.reshape(KT, P, P).transpose(1, 0, 2).reshape(1, P, KT * P))
    parts += [_units(q), _units(k), _units(v)]
    for c in range(4):
        parts += [_units(o[:, c * CW:(c + 1) * CW]), _units(z[:, c * CW:(c + 1) * CW])]
    parts += [_units(zb), _units(cq), _units(ckv), _units(ga), _units(gb)]
    uq = i["w_uq"][0].reshape(LORA, H_B, D_HQK)
    ukv = i["w_ukv"][0].reshape(LORA, H_B, D_NOPE + 128)
    for part in (uq[:, :, :D_NOPE], uq[:, :, D_NOPE:], ukv[:, :, :D_NOPE], ukv[:, :, D_NOPE:]):
        parts.append(_units(part.reshape(LORA, -1)))
    parts += [_units(i["w_a"][0]), _units(i["w_b"][0]), _units(i["w_out"][0])]
    w2 = i["w_in_2"][0]
    parts += [_units(w2[:, 1024:]), _units(w2[:, :1024]), _units(i["w_out_2"][0])]
    for n in range(N_SLABS):
        parts.append(_units(i["w_up_2"][0][:, n * D:(n + 1) * D]))
        parts.append(_units(i["w_down_2"][0][n * D:(n + 1) * D, :]))
    r = np.concatenate(parts, axis=0)
    assert r.shape == (UNITS, P, 2 * PIECE), r.shape
    return r


def _params(i):
    r = np.zeros((P, N_PARAMS), np.float32)
    col = lambda v: v.reshape(-1, P).T
    for name, v in (("norm_g", col(i["norm_g"][0])), ("ml_g", col(i["mlstm_norm_g"][0])),
                    ("q_lat_g", col(i["q_lat_g"][0])), ("kv_lat_g", col(i["kv_lat_g"][0])),
                    ("q_nope_g", col(i["q_norm_g"][0][:P])), ("k_nope_g", col(i["k_norm_g"][0][:P])),
                    ("mix_g", col(i["norm_mix_g_2"][0])), ("mlp_g", col(i["norm_mlp_g_2"][0])),
                    ("conv_w", i["conv_w"][0].reshape(4, 16, P).transpose(2, 1, 0).reshape(P, 64)),
                    ("gate_b", np.broadcast_to(i["gate_bias"][0], (P, 16))),
                    ("q_rope_g", np.broadcast_to(i["q_norm_g"][0][P:], (P, 64))),
                    ("k_rope_g", np.broadcast_to(i["k_norm_g"][0][P:], (P, 64)))):
        r[:, PARAMS[name]] = v
    return r


def _consts():
    early = np.zeros((P, N_EARLY), np.float32)
    r = np.zeros((P, N_CONSTS), np.float32)
    n = np.arange(P)
    r[:, CONSTS["ident"]] = np.eye(P)
    ahead = np.where(n[None, :] > n[:, None], -BIG, 0.0)
    r[:, CONSTS["attn_mask"]] = np.concatenate([ahead, np.zeros((P, P)), ahead], axis=1)
    r[:, CONSTS["ml_mask"]] = np.concatenate([np.where(n[:, None] > n[None, :], BIG, 0.0), np.zeros((P, P))], axis=1)
    early[:, EARLY["tri"]] = n[:, None] <= n[None, :]
    early[:, EARLY["ones"]] = 1.0
    e = (np.float32(-np.log(10000.0)) * np.arange(0, D_ROPE, 2, dtype=np.float32)) / np.float32(D_ROPE)
    early[:, EARLY["inv_freq"]] = np.exp(e.astype(np.float64)).astype(np.float32)
    m = np.arange(FD)
    ang = 2 * np.pi * ((m[:, None] * m[None, :]) % FD) / FD
    dft = np.concatenate([np.cos(ang), np.sin(ang), -np.sin(ang)], axis=1).astype(np.float32)
    dft = dft.reshape(2, P, 3 * FD).transpose(1, 0, 2).copy()
    t = np.arange(TOK)
    dist = np.abs(t[:, None] - t[None, :])
    seen = np.zeros((TOK, TOK))
    for window, dil in ((128, 1), (512, 4), (2048, 16)):
        seen += (dist % dil == 0) & (dist // dil <= window // 2 // dil)
    table = np.where(seen > 0, np.log(np.maximum(seen, 1)), -BIG)
    slopes = 2.0 ** (-8.0 * (np.arange(H_2) + 1) / H_2)
    alibi = (table[None] - slopes[:, None, None] * dist[None]).astype(np.float32)
    alibi = alibi.reshape(H_2, 2, P, TOK).transpose(2, 0, 1, 3).reshape(P, H_2, 2 * TOK).copy()
    return r, early, dft, alibi


def kernel(**inputs):
    import concourse.bacc as bacc
    from concourse.bass_utils import run_bass_kernel_spmd

    i = {k: np.asarray(v) for k, v in inputs.items()}
    consts, early, dft, alibi = _consts()
    arrays = {
        "stream": _stream(i),
        "x": np.ascontiguousarray(i["x"][0]),
        "consts": consts,
        "early": early,
        "params": _params(i),
        "pos": np.ascontiguousarray(i["positions"][0].reshape(TT, P).T),
        "dft": dft,
        "alibi": alibi,
        "fg": np.ascontiguousarray(np.broadcast_to(i["norm_final_g_2"], (P, D))),
        "wf": np.ascontiguousarray(i["w_fourier_2"][0].reshape(FG, 2, P, FD).transpose(2, 0, 1, 3)),
    }
    nc = bacc.Bacc("TRN2", target_bir_lowering=False, num_devices=1)
    f32 = mybir.dt.float32
    ap = {n: nc.dram_tensor(n, a.shape, mybir.dt.from_np(a.dtype), kind="ExternalInput").ap() for n, a in arrays.items()}
    stores = [nc.dram_tensor(n, (P, TT, D), f32, kind="Internal").ap() for n in ("z_store", "ga_store", "gb_store")]
    out = nc.dram_tensor("out", (TOK, D), f32, kind="ExternalOutput").ap()
    build(nc, *(ap[n] for n in ("stream", "x", "consts", "early", "params", "pos", "dft", "alibi", "fg", "wf")), *stores, out)
    r = run_bass_kernel_spmd(nc, [arrays], core_ids=[0])
    return r.results[0]["out"].reshape(1, TOK, D)
```

```python
import concourse.bass as bass
from concourse import mybir
from contextlib import ExitStack, contextmanager
import numpy as np

P = 128
TOK, TT = 256, 2
D = 2048
KT = D // P
CW = 512
H_A, DK_A, DV_A = 8, 128, 256
H_B, D_NOPE, D_ROPE, D_HQK = 16, 128, 64, 192
H_2, HD_2 = 8, 128
LORA = 512
FG, FD = 4, 256
N_COS = FD // 2 + 1
N_SLABS = 4
EPS = 1e-6
BIG = 1e30
PIECE = 2 * CW
RING = 4
NORM_FULL = 8
NORM_LORA = 2
UNITS = 1 + 4 * (4 + 4 + 8 + 4 + 2 + 8) + 14 + 4 * (4 + 4 + 4) + 4 * 8 + 4 * 4 + 4 * N_SLABS * 8

CONSTS = {}
PARAMS = {}


def _columns(table, names):
    at = 0
    for name, n in names:
        table[name] = slice(at, at + n)
        at += n
    return at


N_CONSTS = _columns(CONSTS, [("ident", 128), ("attn_mask", 384), ("ml_mask", 256)])
EARLY = {}
N_EARLY = _columns(EARLY, [("tri", 128), ("ones", 128), ("inv_freq", 32)])
N_PARAMS = _columns(PARAMS, [("norm_g", 16), ("ml_g", 16), ("q_lat_g", 4), ("kv_lat_g", 4), ("q_nope_g", 1),
                             ("k_nope_g", 1), ("mix_g", 16), ("mlp_g", 16), ("conv_w", 64), ("gate_b", 16),
                             ("q_rope_g", 64), ("k_rope_g", 64)])


LATENT = ("r0", "v0", "r1", "v1", "k0", "v2", "k1", "v3", "k2", "q0", "k3", "q1", "q2", "q3")


def _latent_groups():
    put = {(c, j): [] for c in range(15) for j in range(8)}
    for c, name in enumerate(LATENT):
        kind, m = name[0], int(name[1])
        later = {"r": (4, 5), "k": (3, 4, 5), "q": (0, 1), "v": ()}[kind]
        for part, n in enumerate(later):
            put[c + 1 + n // 2, n % 2].append((kind, m, part))
    for g, at in enumerate(((8, 0), (9, 0), (13, 0), (13, 1), (14, 0), (14, 1), (14, 3), (14, 4))):
        put[at].append(("a", 0, g))
    return put


LATENT_GROUPS = _latent_groups()


class Tally:

    def __init__(self):
        self.n, self.reg, self.step = 0, None, 0

    def add(self, k=1):
        self.n += k

    def at(self, ahead=0):
        v = self.n + ahead
        return v if self.reg is None else self.reg * self.step + v

    def cycle(self, period):
        v = self.n // period + 1
        return v if self.reg is None else self.reg * (self.step // period) + v


@contextmanager
def loop(eng, count, steps):
    with eng.Fori(0, count) as i:
        first = {t: t.n for t in steps}
        for t, k in steps.items():
            t.reg, t.step = i, k
        yield i
    for t, k in steps.items():
        assert t.n == first[t] + k, (t.n - first[t], k)
        t.n, t.reg = first[t] + count * k, None


def build(nc, stream, x_in, consts_in, early_in, params_in, pos_in, dft_in, alibi_in, fg_in, wf_in, z_store, ga_store, gb_store,
          out):
    f32, f32r, i32 = mybir.dt.float32, mybir.dt.float32r, mybir.dt.int32
    ALU, ACT, AX = mybir.AluOpType, mybir.ActivationFunctionType, mybir.AxisListType
    MUL, ADD, SUB, MAX, MIN = ALU.mult, ALU.add, ALU.subtract, ALU.max, ALU.min

    ctx = ExitStack()
    with ctx:
        base = 16512
        K = 1024

        def place(name, shape, dt, kb):
            return nc.alloc_sbuf_tensor_at(name, shape, dt, offset=base + int(kb * K))

        raw = place("raw", [P, RING, 2 * PIECE], f32, 0)
        w_hi = place("w_hi", [P, RING, PIECE], f32r, 32)
        w_lo = place("w_lo", [P, RING, PIECE], f32r, 48)
        a_hi = place("a_hi", [P, KT, TOK], f32r, 64)
        a_lo = place("a_lo", [P, KT, TOK], f32r, 80)
        nat = place("nat", [P, TT, D], f32, 96)
        qk_t = place("qk_t", [P, 2 * H_A, TOK], f32, 112)
        v_a = place("v_a", [P, TT, H_A, DV_A + 1], f32, 128)
        lat_hi = place("lat_hi", [P, 8, TOK], f32r, 144.25)
        lat_lo = place("lat_lo", [P, 8, TOK], f32r, 152.25)
        z1 = place("z1", [P, TT, D], f32, 160.25)
        z2 = place("z2", [P, TT, D], f32, 176.25)
        scr = place("scr", [P, D], f32, 160.25)
        qn_t = place("qn_t", [P, H_B, TOK], f32, 112)
        kn_t = place("kn_t", [P, H_B, TOK], f32, 128)
        yb = place("yb", [P, TT, D], f32, 144.25)
        qr_t = place("qr_t", [P, H_B // 2, TOK], f32, 160.25)
        kr_t = place("kr_t", [P, H_B // 2, TOK], f32, 168.25)
        v_b = place("v_b", [P, TT, D], f32, 176.25)
        ga = place("ga", [P, TT, D], f32, 112)
        gb = place("gb", [P, TT, D], f32, 128)
        x_of = {"r0": place("x_r0", [P, TT, CW], f32, 64), "r1": place("x_r1", [P, TT, CW], f32, 72),
                "k0": place("x_k0", [P, TT, CW], f32, 80), "k2": place("x_k2", [P, TT, CW], f32, 76),
                "q0": place("x_q0", [P, TT, CW], f32, 72), "q1": place("x_q1", [P, TT, CW], f32, 76),
                "q2": place("x_q2", [P, TT, CW], f32, 92), "q3": place("x_q3", [P, TT, CW], f32, 76)}
        roped_of = [place("roped0", [P, TT, CW], f32, 68), place("roped1", [P, TT, CW], f32, 76)]
        shared_of = [place(f"shared{m}", [P, TT, 4 * D_ROPE], f32, kb) for m, kb in enumerate((84, 86, 84, 86))]
        rope_b = place("rope_b", [P, TT, CW], f32, 84)
        sq_odd = place("sq_odd", [P, TT, CW], f32, 88)
        sq_last = place("sq_last", [P, TT, CW], f32, 92)
        cos_g = place("cos_g", [P, TT, D_ROPE], f32, 94)
        sin_g = place("sin_g", [P, TT, D_ROPE], f32, 94.5)
        dft = place("dft", [P, 2, 3 * FD], f32, 112)
        wf = place("wf", [P, FG, 2, FD], f32, 118)
        g_sb = place("g_sb", [P, 2, 2, FD], f32, 126)
        cos_part = place("cos_part", [P, 2, N_COS], f32, 130)
        re_sb = place("re_sb", [P, 2, FD], f32, 134)
        y2 = place("y2", [P, TT, H_2 * HD_2], f32, 136)
        q2_t = place("q2_t", [P, H_2, TOK], f32, 144.25)
        k2_t = place("k2_t", [P, H_2, TOK], f32, 152.25)
        v2 = place("v2", [P, TT, H_2 * HD_2], f32, 160.25)
        uf = place("uf", [P, TT, FG * FD], f32, 168.25)
        alibi = place("alibi", [P, H_2, 2 * TOK], f32, 176.25)
        m_hi = place("m_hi", [P, KT, TOK], f32r, 112)
        m_lo = place("m_lo", [P, KT, TOK], f32r, 128)
        fg = place("fg", [P, D], f32, 144.25)
        e_at = 180.25
        early = place("early", [P, N_EARLY], f32, e_at)
        mrow = place("mrow", [8, 2, P + TOK], f32, e_at + 2)
        sm = place("sm", [P, TT, 80], f32, e_at + 5)
        tmp = place("tmp", [P, TT, 32], f32, e_at + 6)
        f_nat = place("f_nat", [P, TT, 8], f32, e_at + 7)
        lf = place("lf", [P, TT, 8], f32, e_at + 7.25)
        at = 192.25
        cst = place("cst", [P, N_CONSTS], f32, at)
        at += N_CONSTS * 4 / K
        par = place("par", [P, N_PARAMS], f32, at)
        at += N_PARAMS * 4 / K
        at = -(-at * K // 32) * 32 / K
        stg = place("stg", [P, TT, CW], f32, at)
        stg2 = place("stg2", [P, TT, CW], f32, at + 4)
        at += 8
        x_of["k1"] = x_of["k3"] = stg
        squares_of = {"r0": stg2, "r1": sq_odd, "k0": stg2, "k1": sq_odd, "k2": stg2, "q0": sq_odd, "k3": stg2,
                      "q1": sq_odd, "q2": stg2, "q3": sq_last}

        def little(name, shape, dt=f32):
            nonlocal at
            n = 1
            for s in shape[1:]:
                n *= s
            t = place(name, shape, dt, at)
            at += -(-n * 4 // 32) * 32 / K
            return t

        neg_half = little("neg_half", [P, 32])
        kr = little("kr", [P, TT, 64])
        cos = little("cos", [P, TT, 32])
        sin = little("sin", [P, TT, 32])
        m_fin = little("m_fin", [8, TOK])
        a_nat = little("a_nat", [P, TT, 8])
        expm = little("expm", [P, TT, 8])
        pos_i = little("pos_i", [P, TT], i32)
        pos_f = little("pos_f", [P, TT])
        ss1 = little("ss1", [P, TT])
        ms1 = little("ms1", [P, TT])
        inv1 = little("inv1", [P, TT])
        ss_l = little("ss_l", [P, 2, TT])
        ms_l = little("ms_l", [P, 2, TT])
        inv_l = little("inv_l", [P, 2, TT])
        ml_ss = little("ml_ss", [P, TT])
        ml_r = little("ml_r", [P, TT])
        ml_t = little("ml_t", [P, TT])
        ml_ms = little("ml_ms", [P, TT])
        ml_f = little("ml_f", [P, TT])
        ss_kr = little("ss_kr", [P, TT])
        ss_q = little("ss_q", [P, TT, H_B])
        ss_qr = little("ss_qr", [P, TT, H_B])
        inv_q = little("inv_q", [P, TT, H_B])
        ss_k = little("ss_k", [P, TT, 4])
        inv_k = little("inv_k", [P, TT, 4])
        nmax = little("nmax", [P, 2, TT])
        nb = little("nb", [P, 2, TT])
        den = little("den", [P, 2, TT])
        rden = little("rden", [P, TT])
        ss2 = little("ss2", [P, TT, 4])
        inv2 = little("inv2", [P, TT])
        inv3 = little("inv3", [P, TT])
        inv4 = little("inv4", [P, TT])
        assert base + at * K <= nc.sbuf_usable_end, (at, nc.sbuf_usable_end)

        def psum(name, shape=(P, 512)):
            return ctx.enter_context(nc.psum_tensor(name, list(shape), f32))

        proj = [psum(f"proj{i}") for i in range(4)]
        tbank = [psum(f"tbank{i}") for i in range(2)]
        bank_a = psum("bank_a")
        bank_b = psum("bank_b")
        x_banks = tbank + [proj[2], proj[3], bank_a, bank_b] + tbank

        ident = cst[:, CONSTS["ident"]]

        def par_c(name, i=0):
            s = PARAMS[name]
            return par[:, s.start + i:s.start + i + 1]

        def sem(name):
            return ctx.enter_context(nc.semaphore(name))

        raw_landed = [sem(f"raw_landed{i}") for i in range(RING)]
        w_rounded = sem("w_rounded")
        w_rest = sem("w_rest")
        w_used = sem("w_used")
        proj_read = sem("proj_read")
        t_done = sem("t_done")
        t_hi = sem("t_hi")
        t_by_act = sem("t_by_act")
        t_by_dve = sem("t_by_dve")
        x_ready = [sem(f"x_ready{i}") for i in range(4)]
        ident_ready = sem("ident_ready")
        small_t = sem("small_t")
        cst_ready = sem("cst_ready")
        early_ready = sem("early_ready")
        par_ready = sem("par_ready")
        pos_ready = sem("pos_ready")
        dve_seq = sem("dve_seq")
        act_seq = sem("act_seq")
        pow_asked = sem("pow_asked")
        pow_done = sem("pow_done")
        pool_init = sem("pool_init")
        staged = sem("staged")
        sumsq = sem("sumsq")
        trig_arg = sem("trig_arg")
        trig = sem("trig")
        gate_in = sem("gate_in")
        gate_ln = sem("gate_ln")
        lf_ready = sem("lf_ready")
        f_sum = sem("f_sum")
        a_ready = sem("a_ready")
        a_row = sem("a_row")
        m_row = sem("m_row")
        m_col = sem("m_col")
        m_sum = sem("m_sum")
        m_exp = sem("m_exp")
        conv_done = sem("conv_done")
        conv_sig = sem("conv_sig")
        qk_ready = sem("qk_ready")
        sig = sem("sig")
        gated = sem("gated")
        z_out = sem("z_out")
        z_full = sem("z_full")
        v_ready = sem("v_ready")
        ml_s = sem("ml_s")
        ml_e = sem("ml_e")
        ml_w = sem("ml_w")
        ml_p = sem("ml_p")
        ml_o = sem("ml_o")
        ml_q = sem("ml_q")
        ml_done = sem("ml_done")
        squared = sem("squared")
        roped = sem("roped")
        k_scaled = sem("k_scaled")
        yb_in = [sem(f"yb_in{i}") for i in range(4)]
        s_done = sem("s_done")
        s_read = sem("s_read")
        b_ready = sem("b_ready")
        p_ready = sem("p_ready")
        o_done = sem("o_done")
        o_read = sem("o_read")
        g_in = [sem("ga_in"), sem("gb_in")]
        x_again = sem("x_again")
        res_ready = sem("res_ready")
        alibi_in_s = sem("alibi_in_s")
        dft_in_s = sem("dft_in_s")
        uf_ready = sem("uf_ready")
        f_g = sem("f_g")
        f_ge = sem("f_ge")
        f_r = sem("f_r")
        f_re = sem("f_re")
        f_y = sem("f_y")
        f_hi = sem("f_hi")
        f_lo = sem("f_lo")
        relu = sem("relu")
        fg_in_s = sem("fg_in_s")
        weighted = sem("weighted")
        out_ready = sem("out_ready")
        out_ready_act = sem("out_ready_act")
        stored = sem("stored")

        GATED_IN = 2 + 8 + 8

        def wait(eng, s, value):
            if not isinstance(value, int) or value > 0:
                eng.wait_ge(s, value)

        x_v = x_in.rearrange("(t p) d -> p t d", p=P)
        out_v = out.rearrange("(t p) d -> p t d", p=P)
        block = ctx.enter_context(nc.Block())

        PIECES = 2 * UNITS

        @block.sync
        def _(sp):
            ident_cols = CONSTS["ident"]
            sp.dma_start(cst[:, ident_cols], consts_in[:, ident_cols]).then_inc(ident_ready, 16)
            for c in range(4):
                if c == 2:
                    sp.dma_start(raw[:, 0, :], stream[0]).then_inc(raw_landed[0], 16)
                cols = slice(c * CW, (c + 1) * CW)
                sp.dma_start(nat[:, :, cols], x_v[:, :, cols]).then_inc(x_ready[c], 16)
            sp.dma_start(raw[:, 1, :], stream[1]).then_inc(raw_landed[1], 16)
            sp.dma_start(early[:, :], early_in).then_inc(early_ready, 16)
            for u in range(2, RING):
                sp.dma_start(raw[:, u, :], stream[u]).then_inc(raw_landed[u], 16)
            sp.dma_start(cst[:, ident_cols.stop:], consts_in[:, ident_cols.stop:]).then_inc(cst_ready, 16)
            whole, rest = divmod(UNITS - RING, RING)
            with sp.Fori(0, whole) as i:
                for j in range(RING):
                    sp.wait_ge(w_rest, i * (2 * RING) + 2 * j + 2)
                    sp.dma_start(raw[:, j, :], stream[bass.ds(i * RING + (RING + j), 1)].rearrange("o p n -> (o p) n")
                                 ).then_inc(raw_landed[j], 16)
            for j in range(rest):
                sp.wait_ge(w_rest, 2 * RING * whole + 2 * j + 2)
                sp.dma_start(raw[:, j, :], stream[RING * (whole + 1) + j]).then_inc(raw_landed[j], 16)
            for t, c in ((0, 0), (1, 0), (0, 1), (1, 1), (0, 2), (1, 2), (0, 3), (1, 3)):
                if t == 0 or c == 3:
                    sp.wait_ge(out_ready, c + t + 1)
                else:
                    sp.wait_ge(out_ready_act, c + 1)
                cols = slice(c * CW, (c + 1) * CW)
                sp.dma_start(out_v[:, t, cols], nat[:, t, cols]).then_inc(stored, 16)
            sp.wait_ge(stored, 16 * 8)

        @block.gpsimd
        def _(pool):
            pool.dma_start(par[:, :], params_in).then_inc(par_ready, 16)
            pool.dma_start(pos_i[:, :], pos_in).then_inc(pos_ready, 16)
            nc.gpsimd.memset(neg_half[:, :], -0.5).then_inc(pool_init, 1)
            nc.gpsimd.memset(v_a[:, :, :, DV_A:DV_A + 1], 1.0).then_inc(pool_init, 1)
            nc.gpsimd.memset(mrow[:, :, 0:P], 0.0).then_inc(pool_init, 1)
            pool.wait_ge(pool_init, 1)
            asked = Tally()

            def power(dst, src, width):
                asked.add()
                pool.wait_ge(pow_asked, asked.at())
                nc.gpsimd.tensor_tensor(dst, src, neg_half[:, 0:width], ALU.pow).then_inc(pow_done, 1)

            flat = lambda ap: ap.rearrange("p a b -> p (a b)")
            power(inv1[:, :], ms1[:, :], TT)
            pool.wait_ge(z_full, 1)
            pool.dma_start(z_store, z1[:, :, :]).then_inc(z_out, 16)
            power(flat(inv_l[:, :, :]), flat(ms_l[:, :, :]), 2 * TT)
            for h in range(4):
                power(ml_f[:, :], ml_ms[:, :], TT)
            pool.wait_ge(z_full, 2)
            pool.dma_start(ga_store, z2[:, :, :]).then_inc(z_out, 16)
            for h in range(4, H_A):
                power(ml_f[:, :], ml_ms[:, :], TT)
                pool.wait_ge(z_full, 3 + h - 4)
                c = slice((h - 4) * CW, (h - 3) * CW)
                pool.dma_start(gb_store[:, :, c], z1[:, :, c]).then_inc(z_out, 16)
            for name in LATENT:
                h = slice(4 * int(name[1]), 4 * int(name[1]) + 4)
                if name[0] == "k":
                    power(flat(inv_k[:, :, :]), flat(ss_k[:, :, :]), TT * 4)
                if name[0] == "q":
                    asked.add()
                    pool.wait_ge(pow_asked, asked.at())
                    nc.gpsimd.tensor_tensor(inv_q[:, :, h], ss_q[:, :, h],
                                            neg_half[:, 0:TT * 4].rearrange("p (t h) -> p t h", t=TT),
                                            ALU.pow).then_inc(pow_done, 1)
            pool.wait_ge(w_used, RING + 2 * (1 + 4 * 30 + 14))
            for c in range(4):
                cols = slice(c * CW, (c + 1) * CW)
                pool.dma_start(yb[:, :, cols], z_store[:, :, cols]).then_inc(yb_in[c], 16)
            pool.wait_ge(s_done, H_B)
            pool.dma_start(ga[:, :, :], ga_store).then_inc(g_in[0], 16)
            pool.dma_start(gb[:, :, :], gb_store).then_inc(g_in[1], 16)
            pool.wait_ge(w_used, RING + 2 * (1 + 4 * 30 + 14 + 4 * 8) + 1)
            pool.dma_start(yb[:, :, :], x_v).then_inc(x_again, 16)
            pool.wait_ge(gated, GATED_IN + 8)
            pool.dma_start(alibi[:, :, :], alibi_in).then_inc(alibi_in_s, 16)
            pool.dma_start(dft[:, :, :], dft_in).then_inc(dft_in_s, 16)
            pool.dma_start(wf[:, :, :, :], wf_in).then_inc(dft_in_s, 16)
            power(inv2[:, :], ms1[:, :], TT)
            power(inv3[:, :], ms1[:, :], TT)
            pool.wait_ge(s_done, H_B + H_2)
            pool.dma_start(fg[:, :], fg_in).then_inc(fg_in_s, 16)
            power(inv4[:, :], ms1[:, :], TT)

        @block.tensor
        def _(pe):
            piece, chunk, tr = Tally(), Tally(), Tally()
            by_act, by_dve = Tally(), Tally()
            used = {by_act: t_by_act, by_dve: t_by_dve}
            readers = []

            def group(src, by, n=4):
                if len(readers) > 1:
                    pe.wait_ge(used[readers[-2]], readers[-2].at(-1 if readers[-1] is readers[-2] else 0))
                readers.append(by)
                by.add()
                for b in range(n):
                    last = nc.tensor.transpose(tbank[tr.n % 2][:, b * P:(b + 1) * P], src(b), ident)
                last.then_inc(t_done, 1)
                tr.add()

            def from_nat(buf, g):
                return lambda b: buf[:, b % 2, (2 * g + b // 2) * P:(2 * g + b // 2 + 1) * P]

            def project(hi, lo, k0=0, pieces=NORM_FULL, slot=None, before=None):
                banks = [proj[2 * (chunk.n % 2) + t] for t in range(TT)]
                wait(pe, proj_read, chunk.at(-1) * 2)
                for j in range(pieces):
                    if before:
                        before(j)
                    pe.wait_ge(w_rest, piece.at(1))
                    s = piece.n % RING
                    for k in range(2):
                        kt = k0 + 2 * j + k
                        wh, wl = w_hi[:, s, k * CW:(k + 1) * CW], w_lo[:, s, k * CW:(k + 1) * CW]
                        for t in range(TT):
                            ah, al = hi[:, kt, t * P:(t + 1) * P], lo[:, kt, t * P:(t + 1) * P]
                            first, end = j == 0 and k == 0, j == pieces - 1 and k == 1
                            nc.tensor.matmul(banks[t][:, :], ah, wh, start=first, stop=False)
                            nc.tensor.matmul(banks[t][:, :], ah, wl, start=False, stop=False)
                            last = nc.tensor.matmul(banks[t][:, :], al, wh, start=False, stop=end)
                    last.then_inc(w_used, 1)
                    piece.add()
                    if slot:
                        slot(j)
                chunk.add()

            def turn(buf, ready):
                first = []

                def put(g):
                    if not first:
                        first.append(by_dve.n)
                    ready(g)
                    group(from_nat(buf, g), by_dve)

                def tail(j):
                    if 1 <= j <= 6:
                        put(j - 1)

                def head(j):
                    if 2 <= j <= 3:
                        put(j + 4)

                def before(j):
                    pe.wait_ge(t_by_dve, first[0] + j + 1)
                return tail, head, before

            pe.sem_inc(w_used, RING)
            pe.wait_ge(ident_ready, 16)
            for g in range(8):
                if g % 2 == 0:
                    pe.wait_ge(x_ready[g // 2], 16)
                if g >= 6:
                    pe.wait_ge(t_by_dve, g - 5)
                for b in range(4):
                    last = nc.tensor.transpose(x_banks[g][:, b * P:(b + 1) * P], from_nat(nat, g)(b), ident)
                last.then_inc(t_done, 1)
            readers += [by_dve] * 8
            by_dve.add(8)
            tr.add(8)

            for j in range(2):
                pe.wait_ge(t_by_dve, 4 * j + 4)
                pe.wait_ge(w_rest, piece.at(1))
                s = piece.n % RING
                for k in range(8):
                    kt = 8 * j + k
                    wh, wl = w_hi[:, s, k * P:(k + 1) * P], w_lo[:, s, k * P:(k + 1) * P]
                    o = proj[0][:, 0:TOK]
                    nc.tensor.matmul(o, wh, a_hi[:, kt, :], start=(kt == 0), stop=False)
                    nc.tensor.matmul(o, wh, a_lo[:, kt, :], start=False, stop=False)
                    last = nc.tensor.matmul(o, wl, a_hi[:, kt, :], start=False, stop=(kt == KT - 1))
                last.then_inc(w_used, 1)
                piece.add()
            chunk.add()

            def gates_slot(j):
                tri, ones = early[:, EARLY["tri"]], early[:, EARLY["ones"]]
                if j == 0:
                    pe.wait_ge(proj_read, 2)
                    for t in range(TT):
                        last = nc.tensor.transpose(bank_b[:, t * P:(t + 1) * P], stg2[:, 0, t * P:(t + 1) * P], ident)
                    last.then_inc(small_t, 1)
                if j == 2:
                    pe.wait_ge(lf_ready, 1)
                    pe.wait_ge(early_ready, 16)
                    nc.tensor.matmul(bank_a[:, 0:8], tri, lf[:, 0, :], start=True, stop=True)
                    nc.tensor.matmul(bank_a[:, 8:16], ones, lf[:, 0, :], start=True, stop=False)
                    nc.tensor.matmul(bank_a[:, 8:16], tri, lf[:, 1, :], start=False, stop=True).then_inc(f_sum, 1)
                if j == 3:
                    pe.wait_ge(a_ready, 1)
                    for t in range(TT):
                        last = nc.tensor.transpose(bank_b[0:8, t * P:(t + 1) * P], a_nat[:, t, :], ident)
                    last.then_inc(a_row, 1)
                if j == 7:
                    pe.wait_ge(m_row, 1)
                    for t in range(TT):
                        last = nc.tensor.transpose(bank_a[:, 16 + 8 * t:24 + 8 * t], m_fin[:, t * P:(t + 1) * P],
                                                   cst[0:8, 0:8])
                    last.then_inc(m_col, 1)

            def stg_slot(j, n, by=by_dve, at=(1, 2)):
                if j == 1:
                    pe.wait_ge(staged, n)
                if j in at:
                    group(from_nat(stg, at.index(j)), by)

            project(a_hi, a_lo, slot=gates_slot)
            for i in range(1, 4):
                project(a_hi, a_lo, slot=lambda j: stg_slot(j, i, at=(1, 3)))
            project(a_hi, a_lo, slot=lambda j: stg_slot(j, 4, at=(1, 3)))
            for i in range(3):
                project(a_hi, a_lo)
            with loop(pe, 6, {piece: 16, chunk: 2}):
                project(a_hi, a_lo)
                project(a_hi, a_lo)
            project(a_hi, a_lo)
            project(a_hi, a_lo, slot=lambda j: stg_slot(j, 5))

            def mlstm_slot(h):
                def slot(j):
                    if h == 0:
                        stg_slot(j, 6)
                    if j == 1:
                        if h == 0:
                            pe.wait_ge(qk_ready, 8)
                            pe.wait_ge(m_row, 1)
                        wait(pe, ml_done, h)
                        q, k = qk_t[:, h, :], qk_t[:, H_A + h, :]
                        nc.tensor.matmul(bank_a[:, 0:TOK], k[:, 0:P], q, start=True, stop=True)
                        nc.tensor.matmul(bank_a[:, TOK:TOK + P], k[:, P:TOK], q[:, P:TOK], start=True, stop=True)
                        nc.tensor.matmul(bank_b[:, 0:TOK], cst[0:8, h:h + 1].to_broadcast([8, P]), m_fin[:, :],
                                         start=True, stop=True).then_inc(ml_s, 1)
                    if j == 4:
                        pe.wait_ge(ml_p, h + 1)
                        if h == 0:
                            pe.wait_ge(v_ready, 8)
                            pe.wait_ge(pool_init, 3)
                        pt = stg2[:, 1, 0:384]
                        nc.tensor.matmul(bank_b[:, 0:DV_A + 1], pt[:, 0:P], v_a[:, 0, h, :], start=True, stop=True)
                        nc.tensor.matmul(bank_a[:, 0:DV_A + 1], pt[:, P:2 * P], v_a[:, 0, h, :], start=True, stop=False)
                        nc.tensor.matmul(bank_a[:, 0:DV_A + 1], pt[:, 2 * P:3 * P], v_a[:, 1, h, :], start=False,
                                         stop=True).then_inc(ml_o, 1)
                return slot

            for h in range(H_A):
                project(a_hi, a_lo, slot=mlstm_slot(h))

            a_first = []

            def latent_slot(c, j):
                for kind, m, part in LATENT_GROUPS[c, j]:
                    if kind == "r":
                        if part == 0:
                            pe.wait_ge(roped, m + 1)
                        group(from_nat(roped_of[m], part), by_act)
                    elif kind == "q":
                        if part == 0:
                            pe.wait_ge(proj_read, 2 * chunk.n)
                        group(from_nat(x_of[f"q{m}"], part), by_act)
                    elif kind == "k":
                        if part == 0:
                            pe.wait_ge(k_scaled, m + 1)
                        group(from_nat(x_of[f"k{m}"], part) if part < 2 else from_nat(shared_of[m], 0), by_act)
                    else:
                        if part == 0:
                            a_first.append(by_dve.n)
                        group(from_nat(nat, part), by_dve)

            pe.wait_ge(ml_done, H_A)

            def scores_b(h):
                wait(pe, s_read, h)
                r = slice(64 * (h % 2), 64 * (h % 2) + 64)
                for t, keys, to in ((0, P, 0), (1, TOK, P)):
                    q = slice(t * P, (t + 1) * P)
                    nc.tensor.matmul(bank_a[:, to:to + keys], qn_t[:, h, q], kn_t[:, h, 0:keys], start=True, stop=False)
                    last = nc.tensor.matmul(bank_a[:, to:to + keys], qr_t[r, h // 2, q], kr_t[r, h // 2, 0:keys],
                                            start=False, stop=True)
                last.then_inc(s_done, 1)

            def probs_b(h):
                pe.wait_ge(p_ready, h + 1)
                group(lambda b: stg[:, h % 2, b * P:(b + 1) * P], by_act, n=3)
                return by_act.n

            def values_b(h, n):
                pe.wait_ge(t_by_act, n)
                wait(pe, o_read, h)
                pt = stg2[:, h % 2, 0:384]
                v0, v1 = v_b[:, 0, h * P:(h + 1) * P], v_b[:, 1, h * P:(h + 1) * P]
                nc.tensor.matmul(bank_b[:, 0:P], pt[:, 0:P], v0, start=True, stop=True)
                nc.tensor.matmul(bank_b[:, P:2 * P], pt[:, P:2 * P], v0, start=True, stop=False)
                nc.tensor.matmul(bank_b[:, P:2 * P], pt[:, 2 * P:3 * P], v1, start=False, stop=True).then_inc(o_done, 1)

            t_of = {}

            def heads_b(n):
                h, odd = divmod(n, 2)
                if odd and h >= 0:
                    if h == 0:
                        pe.wait_ge(proj_read, 2 * 45)
                    values_b(h, t_of[h])
                if not odd:
                    if h >= 0:
                        t_of[h] = probs_b(h)
                    if h + 1 < H_B:
                        scores_b(h + 1)

            for c, name in enumerate(LATENT):
                def slot(j, c=c):
                    latent_slot(c, j)
                    if c == 13:
                        heads_b(j - 2)
                project(lat_hi, lat_lo, k0=0 if name[0] in "rq" else 4, pieces=NORM_LORA, slot=slot)

            def a_before(j):
                pe.wait_ge(t_by_dve, a_first[0] + j + 1)

            b_tail, b_head, b_before = turn(yb, lambda g: pe.wait_ge(o_read, 2 * g + 2))
            for c in range(4):
                def slot(j, c=c):
                    if c == 0:
                        latent_slot(14, j)
                    heads_b(8 * c + j)
                    if c == 3:
                        b_tail(j)
                project(a_hi, a_lo, slot=slot, before=a_before if c == 0 else None)

            def projection(head, before, tail):
                project(a_hi, a_lo, slot=head, before=before)
                project(a_hi, a_lo)
                project(a_hi, a_lo)
                project(a_hi, a_lo, slot=tail)

            y_tail, y_head, y_before = turn(nat, lambda g: pe.wait_ge(gated, GATED_IN + 2 * (g // 2 + 1)))
            projection(b_head, b_before, y_tail)
            r_tail, r_head, r_before = turn(nat, lambda g: pe.wait_ge(res_ready, 2 * (g // 2 + 1)))
            projection(y_head, y_before, r_tail)
            project(a_hi, a_lo, slot=r_head, before=r_before)
            for i in range(4):
                project(a_hi, a_lo, slot=lambda j: stg_slot(j, 7 + i, by_act))

            def scores_2(h):
                wait(pe, s_read, H_B + h)
                if h == 0:
                    pe.wait_ge(t_by_act, by_act.n)
                for t in range(TT):
                    last = nc.tensor.matmul(bank_a[:, t * TOK:(t + 1) * TOK], q2_t[:, h, t * P:(t + 1) * P], k2_t[:, h, :],
                                            start=True, stop=True)
                last.then_inc(s_done, 1)

            def probs_2(h):
                pe.wait_ge(p_ready, H_B + h + 1)
                group(lambda b: stg[:, h % 2, b * P:(b + 1) * P], by_act)
                return by_act.n

            def values_2(h, n):
                pe.wait_ge(t_by_act, n)
                wait(pe, o_read, H_B + h)
                pt = stg2[:, h % 2, :]
                for t in range(TT):
                    for kt in range(2):
                        b = 2 * t + kt
                        last = nc.tensor.matmul(bank_b[:, t * P:(t + 1) * P], pt[:, b * P:(b + 1) * P],
                                                v2[:, kt, h * P:(h + 1) * P], start=(kt == 0), stop=(kt == 1))
                last.then_inc(o_done, 1)

            def heads_2(n):
                h, odd = divmod(n, 2)
                if odd and h >= 0:
                    if h == 0:
                        pe.wait_ge(proj_read, 2 * (45 + 12 + 6))
                    values_2(h, t_of[h])
                if not odd:
                    if h >= 0:
                        t_of[h] = probs_2(h)
                    if h + 1 < H_2:
                        scores_2(h + 1)

            project(a_hi, a_lo, slot=lambda j: heads_2(j - 8) if j >= 6 else None)
            y2_first = by_dve.n
            for c in range(2):
                def slot(j, c=c):
                    heads_2(8 * c + j)
                    if c and j >= 5:
                        pe.wait_ge(o_read, H_B + 2 * (j - 5) + 2)
                        group(from_nat(y2, j - 5), by_dve)
                project(a_hi, a_lo, slot=slot)

            def positions_dft(g):
                for ct in range(2):
                    for kt in range(2):
                        last = nc.tensor.matmul(proj[g][:, ct * FD:(ct + 1) * FD],
                                                uf[:, kt, g * FD + ct * P:g * FD + (ct + 1) * P],
                                                dft[:, kt, 0:FD], start=(kt == 0), stop=(kt == 1))
                last.then_inc(f_g, 1)

            def channels_dft(g):
                pe.wait_ge(f_ge, g + 1)
                wait(pe, f_re, g)
                if g == 0:
                    pe.wait_ge(s_read, H_B + H_2)
                for c2 in range(2):
                    for part, ks in enumerate((slice(0, N_COS), slice(N_COS, FD))):
                        for ct in range(2):
                            table = (1 + part) * FD + c2 * P
                            last = nc.tensor.matmul(bank_a[:, c2 * FD + ks.start:c2 * FD + ks.stop],
                                                    dft[:, ct, table:table + P], g_sb[:, g % 2, ct, ks],
                                                    start=(ct == 0), stop=(ct == 1))
                last.then_inc(f_r, 1)

            def fourier_map(g):
                pe.wait_ge(f_re, g + 1)
                wait(pe, f_lo, g)
                if g == 0:
                    pe.wait_ge(o_read, H_B + H_2)
                for e2 in range(2):
                    for c2 in range(2):
                        last = nc.tensor.matmul(bank_b[:, e2 * FD:(e2 + 1) * FD], wf[:, g, c2, e2 * P:(e2 + 1) * P],
                                                re_sb[:, c2, :], start=(c2 == 0), stop=(c2 == 1))
                last.then_inc(f_y, 1)

            pe.wait_ge(proj_read, chunk.at() * 2)
            pe.wait_ge(dft_in_s, 32)
            positions_dft(0)
            positions_dft(1)
            for g in range(FG):
                channels_dft(g)
                if g + 2 < FG:
                    positions_dft(g + 2)
                if g == 2:
                    group(from_nat(y2, 3), by_dve)
                if g + 1 < FG:
                    fourier_map(g)
            def mix_before(j):
                if j < 4:
                    pe.wait_ge(t_by_dve, y2_first + j + 1)
                else:
                    pe.wait_ge(f_lo, j - 3)

            def mix_slot(j):
                if j == 0:
                    fourier_map(FG - 1)

            m_tail, m_head, m_before = turn(nat, lambda g: pe.wait_ge(res_ready, 8 + 2 * (g // 2 + 1)))
            projection(mix_slot, mix_before, m_tail)
            up = Tally()

            def hidden_slot(j):
                if j == 1:
                    pe.wait_ge(relu, up.at() * 2)
                if 1 <= j <= 2:
                    group(from_nat(stg, j - 1), by_dve)

            def hidden_before(j):
                if j == 0 or j == 6:
                    pe.wait_ge(t_by_dve, by_dve.at())

            def slab(head=None, before=None):
                project(a_hi, a_lo, slot=head, before=before)
                for j in range(3):
                    up.add()
                    project(a_hi, a_lo, slot=hidden_slot)
                up.add()
                project(m_hi, m_lo, slot=hidden_slot, before=hidden_before)
                for j in range(3):
                    project(m_hi, m_lo)

            slab(m_head, m_before)
            with loop(pe, N_SLABS - 1, {piece: 64, chunk: 8, tr: 8, by_dve: 8, up: 4}):
                slab()
            assert piece.n == PIECES, (piece.n, PIECES)

        @block.scalar
        def _(act):
            piece, done, chunk, tr, seq = Tally(), Tally(), Tally(), Tally(), Tally()
            sums = Tally()
            A = nc.scalar.activation

            def chain(ins):
                ins.then_inc(act_seq, 1)
                seq.add()
                act.wait_ge(act_seq, seq.at())

            def split(n=1):
                for _ in range(n):
                    if piece.reg is None and piece.n >= PIECES:
                        return
                    u = piece.n // 2
                    if piece.n % 2 == 0:
                        act.wait_ge(raw_landed[u % RING], piece.cycle(2 * RING) * 16)
                    act.wait_ge(w_used, piece.at(1))
                    A(w_hi[:, piece.n % RING, :], raw[:, u % RING, (piece.n % 2) * PIECE:(piece.n % 2 + 1) * PIECE],
                      ACT.Copy).then_inc(w_rounded, 1)
                    piece.add()

            def pieces(n=NORM_FULL, slot=None, ahead=True):
                for j in range(n):
                    if ahead:
                        split()
                    if slot:
                        slot(j)
                done.add(n)

            def banks():
                act.wait_ge(w_used, done.at(RING))
                b = [proj[2 * (chunk.n % 2) + t] for t in range(TT)]
                chunk.add()
                return b

            def transposed(banks=tbank):
                act.wait_ge(t_done, tr.at(1))
                b = banks[tr.n % len(banks)]
                tr.add()
                return b

            def high(dst, kt, g=None, i=0, banks=tbank):
                b = transposed(banks)
                if g is None:
                    last = A(dst[:, kt:kt + 2, :].rearrange("p a b -> p (a b)"), b[:, :], ACT.Copy)
                else:
                    for f in range(2):
                        last = A(dst[:, kt + f, :], b[:, f * TOK:(f + 1) * TOK], ACT.Copy, scale=par_c(g, i + f))
                last.then_inc(t_hi, 1)

            def square_sum(junk, src, dst):
                wait(act, sumsq, sums.at())
                A(junk, src, ACT.Square, accum_out=dst).then_inc(sumsq, 1)
                sums.add()

            act.wait_ge(par_ready, 16)
            for g in range(8):
                if g in (4, 6):
                    split()
                high(a_hi, 2 * g, "norm_g", 2 * g, x_banks)
            square_sum(scr[:, :], nat[:, 0, :], ss1[:, 0:1])
            split(3)
            square_sum(scr[:, :], nat[:, 1, :], ss1[:, 1:2])
            split()
            done.add(2)
            A(stg2[:, 0, 0:TOK], banks()[0][:, 0:TOK], ACT.Copy).then_inc(proj_read, 2)

            def exp_slot(j):
                if j == 1:
                    act.wait_ge(gate_in, 1)
                    chain(A(lf[:, :, :], lf[:, :, :], ACT.Exp))
                    A(lf[:, :, :], lf[:, :, :], ACT.Ln, bias=1.0).then_inc(gate_ln, 1)
                if j == 7:
                    act.wait_ge(m_sum, 1)
                    A(expm[:, :, :], expm[:, :, :], ACT.Exp, scale=-1.0).then_inc(m_exp, 1)

            acc = [stg2[:, j, :] for j in range(2)]
            sgm = [z2[:, 0, j * CW:(j + 1) * CW] for j in range(2)]

            def conv_slot(j):
                if j in (2, 4):
                    tr.add()
                    act.wait_ge(conv_done, tr.at(-8))
                    A(sgm[j // 2 - 1], acc[j // 2 - 1], ACT.Sigmoid).then_inc(conv_sig, 1)

            def stage(inv, n):
                for t, b in enumerate(banks()):
                    last = A(stg[:, t, :], b[:, :], ACT.Copy, scale=inv[:, t:t + 1])
                    last.then_inc(proj_read, 1)
                act.wait_ge(proj_read, chunk.at() * 2)
                act.sem_inc(staged, 1)

            act.wait_ge(pow_done, 1)
            for i in range(4):
                pieces(slot=exp_slot if i == 0 else conv_slot)
                stage(inv1, i + 1)
            for i in range(4):
                def trig_slot(j, i=i):
                    if i == 2 and j == 4:
                        act.wait_ge(trig_arg, 2)
                        A(sin[:, :, :], sin[:, :, :], ACT.Sin).then_inc(trig, 1)
                        A(cos[:, :, :], cos[:, :, :], ACT.Sin).then_inc(trig, 1)
                pieces(slot=conv_slot if i == 0 else trig_slot)
                for t, b in enumerate(banks()):
                    A(v_a[:, t, 2 * i:2 * i + 2, 0:DV_A], b[:, :].rearrange("p (h d) -> p h d", h=2), ACT.Copy,
                      scale=inv1[:, t:t + 1]).then_inc(proj_read, 1)
            act.wait_ge(proj_read, chunk.at() * 2)
            act.sem_inc(v_ready, 8)
            tiles = Tally()
            with loop(act, 4, {piece: 16, done: 16, chunk: 2, tiles: 2}) as i:
                pieces()
                for t, b in enumerate(banks()):
                    act.wait_ge(gated, tiles.at(2))
                    A(stg[:, t, :], b[:, :], ACT.Sigmoid, scale=inv1[:, t:t + 1]).then_inc(proj_read, 1)
                pieces()
                for t, b in enumerate(banks()):
                    A(stg2[:, t, :], b[:, :], ACT.Sigmoid, scale=inv1[:, t:t + 1]).then_inc(sig, 1)
                tiles.add(2)
            with loop(act, 2, {piece: 16, done: 16, chunk: 2, tiles: 4}) as i:
                for c in range(2):
                    pieces()
                    for t, b in enumerate(banks()):
                        act.wait_ge(gated, tiles.at(2))
                        A(stg[:, t, :], b[:, :], ACT.Sigmoid, scale=inv1[:, t:t + 1]).then_inc(sig, 1)
                    tiles.add(2)
            act.wait_ge(gated, tiles.at(2))
            for i in range(2):
                def lat_slot(j, i=i):
                    if i and 1 <= j <= 2:
                        high(lat_hi, 2 * (j - 1), "q_lat_g", 2 * (j - 1))
                pieces(slot=lat_slot)
                stage(inv1, 5 + i)
                for t in range(TT):
                    square_sum(stg2[:, t, :], stg[:, t, :], ss_l[:, i, t:t + 1])

            for h in range(H_A):
                def slot(j, h=h):
                    if h == 0 and 1 <= j <= 2:
                        high(lat_hi, 2 + 2 * j, "kv_lat_g", 2 * (j - 1))
                    if j == 1:
                        act.wait_ge(ml_e, 2 * h + 2)
                        A(stg2[:, 0, 0:384], stg2[:, 0, 0:384], ACT.Exp, scale=-1.0).then_inc(ml_w, 1)
                    if j == 4:
                        act.wait_ge(ml_o, h + 1)
                        for t, b in enumerate((bank_b, bank_a)):
                            A(stg[:, t, 0:DV_A], b[:, 0:DV_A], ACT.Square, accum_out=ml_ss[:, t:t + 1]).then_inc(ml_q, 1)
                pieces(slot=slot)
                dst = z2 if h < 4 else z1
                if h == 0:
                    act.wait_ge(z_out, 16)
                for t, b in enumerate(banks()):
                    last = A(dst[:, t, (h % 4) * CW:(h % 4 + 1) * CW], b[:, :], ACT.Copy, scale=inv1[:, t:t + 1])
                    last.then_inc(proj_read, 1)
                if h >= 3:
                    act.wait_ge(proj_read, chunk.at() * 2)
                    act.sem_inc(z_full, 1)

            inv_cq, inv_ckv = inv_l[:, 0, :], inv_l[:, 1, :]

            def out_group(dst, scale=None):
                b = transposed()
                src = b[:, :]
                if scale is None:
                    A(dst.rearrange("p a b -> p (a b)"), src, ACT.Copy).then_inc(t_by_act, 1)
                else:
                    A(dst.rearrange("p a b -> p (a b)"), src, ACT.Copy, scale=scale).then_inc(t_by_act, 1)

            act.wait_ge(pow_done, 2)
            act.wait_ge(ml_done, H_A)

            def latent_slot(c, j):
                for kind, m, part in LATENT_GROUPS[c, j]:
                    f = 4 * m + 2 * part
                    if kind == "r":
                        out_group(qr_t[:, f:f + 2, :])
                    elif kind == "q":
                        out_group(qn_t[:, f:f + 2, :], par_c("q_nope_g"))
                    elif kind == "k" and part < 2:
                        out_group(kn_t[:, f:f + 2, :], par_c("k_nope_g"))
                    elif kind == "k":
                        out_group(kr_t[:, 2 * m:2 * m + 2, :])
                    else:
                        if part in (4, 6):
                            act.wait_ge(squared, 6 if part == 4 else 10)
                        high(a_hi, 2 * part, "ml_g", 2 * part)

            def turn_tail(j, g=None):
                if 1 <= j <= 6:
                    high(a_hi, 2 * (j - 1), g, 2 * (j - 1))

            def turn_head(j, g=None):
                if 2 <= j <= 3:
                    high(a_hi, 2 * (j + 4), g, 2 * (j + 4))

            def heads_b(n):
                h, odd = divmod(n, 2)
                if not odd and h >= 0:
                    b = transposed()
                    wait(act, o_done, h - 1)
                    A(stg2[:, h % 2, 0:384], b[:, 0:384], ACT.Copy).then_inc(t_by_act, 1)
                if odd and h + 1 < H_B:
                    h += 1
                    act.wait_ge(b_ready, h + 1)
                    s = stg[:, h % 2, :]
                    A(s[:, 0:P], s[:, 0:P], ACT.Exp, bias=nb[:, h % 2, 0:1], scale=inv_q[:, 0, h:h + 1],
                      accum_out=den[:, h % 2, 0:1])
                    A(s[:, P:384], s[:, P:384], ACT.Exp, bias=nb[:, h % 2, 1:2], scale=inv_q[:, 1, h:h + 1],
                      accum_out=den[:, h % 2, 1:2]).then_inc(p_ready, 1)

            def squares(c):
                if c < 0 or LATENT[c][0] in "vq":
                    return
                name, t0 = LATENT[c], 2 * ((chunk.n - 1) % 2)
                before = sum(other[0] != "v" for other in LATENT[:c])
                wait(act, squared, before - 1)
                for t in range(TT):
                    A(squares_of[name][:, t, :], proj[t0 + t][:, :], ACT.Square,
                      scale=(inv_cq if name[0] in "rq" else inv_ckv)[:, t:t + 1]).then_inc(proj_read, 1)

            for c, name in enumerate(LATENT):
                def slot(j, c=c):
                    if j == 0:
                        squares(c - 1)
                    latent_slot(c, j)
                    if c == 13:
                        heads_b(j - 2)
                pieces(NORM_LORA, slot=slot)
                act.wait_ge(proj_read, chunk.n * 2)
                if name[0] == "v":
                    m = int(name[1])
                    if m == 0:
                        act.wait_ge(z_out, 16 * 6)
                    A(v_b[:, 1, m * CW:(m + 1) * CW], banks()[1][:, :], ACT.Copy, scale=inv_ckv[:, 1:2]).then_inc(proj_read, 1)
                    continue
                if name == "q3":
                    act.wait_ge(squared, 8)
                for t, b in enumerate(banks()):
                    last = A(x_of[name][:, t, :], b[:, :], ACT.Copy, scale=(inv_cq if name[0] in "rq" else inv_ckv)[:, t:t + 1])
                    if name[0] == "q":
                        last.then_inc(proj_read, 1)
            assert chunk.n == 45, chunk.n

            for c in range(4):
                def slot(j, c=c):
                    if c == 0:
                        latent_slot(14, j)
                    heads_b(8 * c + j)
                    if c == 3:
                        turn_tail(j)
                pieces(slot=slot)
                for t, b in enumerate(banks()):
                    A(nat[:, t, c * CW:(c + 1) * CW], b[:, :], ACT.Copy).then_inc(proj_read, 1)
            act.wait_ge(g_in[0], 16)
            act.wait_ge(g_in[1], 16)
            for c in range(4):
                def slot(j, c=c):
                    if c == 0:
                        turn_head(j)
                    if c == 3:
                        turn_tail(j)
                    if j == 6:
                        act.wait_ge(gated, GATED_IN + 2 * c)
                        for t in range(TT):
                            A(stg[:, t, :], ga[:, t, c * CW:(c + 1) * CW], ACT.Sigmoid).then_inc(sig, 1)
                            A(stg2[:, t, :], gb[:, t, c * CW:(c + 1) * CW], ACT.Sigmoid).then_inc(sig, 1)
                pieces(slot=slot)
                chunk.add()
            def res_squares(c, n):
                act.wait_ge(res_ready, n)
                for t in range(TT):
                    square_sum(stg2[:, t, :], nat[:, t, c * CW:(c + 1) * CW], ss2[:, t, c:c + 1])

            for c in range(4):
                def slot(j, c=c):
                    if c == 0:
                        turn_head(j)
                    if c == 3:
                        turn_tail(j, "mix_g")
                    if c and j == 3:
                        res_squares(c - 1, 2 * c)
                pieces(slot=slot)
                chunk.add()
            for i in range(4):
                def slot(j, i=i):
                    if i == 0:
                        turn_head(j, "mix_g")
                        if j == 3:
                            res_squares(3, 8)
                    elif 1 <= j <= 2:
                        dst = (q2_t, k2_t)[(i - 1) // 2]
                        f = 4 * ((i - 1) % 2) + 2 * (j - 1)
                        out_group(dst[:, f:f + 2, :])
                pieces(slot=slot)
                if i == 0:
                    act.wait_ge(pow_done, 19)
                stage(inv2, 7 + i)
            def heads_2(n):
                h, odd = divmod(n, 2)
                if not odd and h >= 0:
                    b = transposed()
                    wait(act, o_done, H_B + h - 1)
                    A(stg2[:, h % 2, :], b[:, :], ACT.Copy).then_inc(t_by_act, 1)
                if odd and h + 1 < H_2:
                    h += 1
                    act.wait_ge(b_ready, H_B + h + 1)
                    s = stg[:, h % 2, :]
                    for t in range(TT):
                        last = A(s[:, t * TOK:(t + 1) * TOK], s[:, t * TOK:(t + 1) * TOK], ACT.Exp,
                                 bias=nmax[:, h % 2, t:t + 1], accum_out=den[:, h % 2, t:t + 1])
                    last.then_inc(p_ready, 1)

            for i in range(2):
                def slot(j, i=i):
                    if i == 0 and 1 <= j <= 2:
                        out_group(k2_t[:, 2 + 2 * j:4 + 2 * j, :])
                    if i == 1 and j >= 6:
                        heads_2(j - 8)
                pieces(slot=slot)
                for t, b in enumerate(banks()):
                    A(v2[:, t, i * CW:(i + 1) * CW], b[:, :], ACT.Copy, scale=inv2[:, t:t + 1]).then_inc(proj_read, 1)
            for c in range(2):
                def slot(j, c=c):
                    heads_2(8 * c + j)
                    if c and 5 <= j < 7:
                        high(a_hi, 2 * (j - 5))
                pieces(slot=slot)
                for t, b in enumerate(banks()):
                    A(uf[:, t, c * CW:(c + 1) * CW], b[:, :], ACT.Copy, scale=inv2[:, t:t + 1]).then_inc(proj_read, 1)
            high(a_hi, 4)
            def dft_out(g):
                wait(act, f_r, g - 1)
                act.wait_ge(f_g, g + 1)
                A(g_sb[:, g % 2, :, :].rearrange("p a b -> p (a b)"), proj[g][:, :], ACT.Copy, scale=1.0 / FD).then_inc(f_ge, 1)

            def mapped(g):
                act.wait_ge(f_y, g + 1)
                A(a_hi[:, 8 + 2 * g:10 + 2 * g, :].rearrange("p a b -> p (a b)"), bank_b[:, :], ACT.Copy).then_inc(f_hi, 1)

            dft_out(0)
            dft_out(1)
            for g in range(FG):
                if g + 2 < FG:
                    dft_out(g + 2)
                if g == 2:
                    high(a_hi, 6)
                if g + 1 < FG:
                    mapped(g)
            for c in range(4):
                def slot(j, c=c):
                    if c == 0 and j == 0:
                        mapped(FG - 1)
                    if c == 3:
                        turn_tail(j, "mlp_g")
                    if c and j == 3:
                        res_squares(c - 1, 8 + 2 * c)
                pieces(slot=slot)
                chunk.add()
            def slab(first=False, end=False):
                for c in range(8):
                    def slot(j, c=c):
                        if 1 <= c <= 4 and 1 <= j <= 2:
                            high(m_hi, 4 * (c - 1) + 2 * (j - 1))
                        if end and c > 4 and j == 3:
                            res_squares(c - 5, 16 + 8 * (N_SLABS - 1) + 2 * (c - 4))
                        if first and c == 0:
                            turn_head(j, "mlp_g")
                            if j == 3:
                                res_squares(3, 16)
                    pieces(slot=slot)
                    if c < 4:
                        if first and c == 0:
                            act.wait_ge(pow_done, 20)
                        for t, b in enumerate(banks()):
                            A(stg[:, t, :], b[:, :], ACT.Relu, scale=inv3[:, t:t + 1]).then_inc(proj_read, 1)
                    else:
                        chunk.add()
            slab(first=True)
            with loop(act, N_SLABS - 2, {piece: 64, done: 64, chunk: 8, tr: 8}):
                slab()
            slab(end=True)
            res_squares(3, 16 + 8 * N_SLABS)
            act.wait_ge(pow_done, 21)
            act.wait_ge(weighted, 3)
            for c in range(3):
                y = nat[:, 1, c * CW:(c + 1) * CW]
                A(y, y, ACT.Copy, scale=inv4[:, 1:2]).then_inc(out_ready_act, 1)

        @block.vector
        def _(dve):
            piece, done, chunk, tr, seq, his = (Tally() for _ in range(6))
            V = nc.vector

            def chain(ins):
                ins.then_inc(dve_seq, 1)
                seq.add()
                dve.wait_ge(dve_seq, seq.at())

            def split(n=1):
                for _ in range(n):
                    if piece.reg is None and piece.n >= PIECES:
                        return
                    dve.wait_ge(w_rounded, piece.at(1))
                    u, s = piece.n // 2, piece.n % RING
                    V.tensor_tensor(w_lo[:, s, :], raw[:, u % RING, (piece.n % 2) * PIECE:(piece.n % 2 + 1) * PIECE],
                                    w_hi[:, s, :].bitcast(f32), SUB).then_inc(w_rest, 1)
                    piece.add()

            def pieces(n=NORM_FULL, slot=None):
                for j in range(n):
                    split()
                    if slot:
                        slot(j)
                done.add(n)

            def banks():
                dve.wait_ge(w_used, done.at(RING))
                b = [proj[2 * (chunk.n % 2) + t] for t in range(TT)]
                chunk.add()
                return b

            def low(hi, lo, kt, g=None, i=0, banks=tbank):
                his.add()
                dve.wait_ge(t_hi, his.at())
                b = banks[tr.n % len(banks)]
                tr.add()
                if g is None:
                    last = V.tensor_tensor(lo[:, kt:kt + 2, :].rearrange("p a b -> p (a b)"), b[:, :],
                                           hi[:, kt:kt + 2, :].rearrange("p a b -> p (a b)").bitcast(f32), SUB)
                else:
                    for f in range(2):
                        last = V.scalar_tensor_tensor(lo[:, kt + f, :], b[:, f * TOK:(f + 1) * TOK], par_c(g, i + f),
                                                      hi[:, kt + f, :].bitcast(f32), MUL, SUB)
                last.then_inc(t_by_dve, 1)

            def mean(dst, src, n):
                V.tensor_scalar(dst, src, 1.0 / n, EPS, MUL, ADD).then_inc(pow_asked, 1)

            dve.sem_inc(gated, 2)
            two_pi = 2 * np.pi
            c1 = 6.28125
            c2 = float(np.float32(np.round((two_pi - c1) * 2 ** 21) / 2 ** 21))
            c3 = float(np.float32(two_pi - c1 - c2))
            magic = 1.5 * 2 ** 23
            pi_f = float(np.nextafter(np.float32(np.pi), np.float32(0)))

            def angles(t):
                if t == 0:
                    dve.wait_ge(pos_ready, 16)
                    chain(V.tensor_copy(pos_f[:, :], pos_i[:, :]))
                ang, k, r = sin[:, t, :], tmp[:, t, :], cos[:, t, :]
                chain(V.tensor_scalar(ang, early[:, EARLY["inv_freq"]], pos_f[:, t:t + 1], None, MUL))
                chain(V.tensor_scalar(k, ang, 1.0 / two_pi, magic, MUL, ADD))
                chain(V.tensor_scalar(k, k, -magic, None, ADD))
                for c in (c1, c2, c3):
                    chain(V.scalar_tensor_tensor(ang, k, -c, ang, MUL, ADD))
                chain(V.tensor_scalar(r, ang, np.pi / 2, None, ADD))
                chain(V.tensor_scalar(k, r, np.pi, -two_pi, ALU.is_gt, MUL))
                chain(V.tensor_tensor(r, r, k, ADD))
                chain(V.tensor_scalar(ang, ang, pi_f, -pi_f, MIN, MAX))
                chain(V.tensor_scalar(r, r, pi_f, -pi_f, MIN, MAX))
                dve.sem_inc(trig_arg, 1)

            dve.wait_ge(par_ready, 16)
            for g in range(8):
                if g in (4, 6):
                    split()
                low(a_hi, a_lo, 2 * g, "norm_g", 2 * g, x_banks)
            split(3)
            dve.wait_ge(sumsq, 2)
            mean(ms1[:, :], ss1[:, :], D)

            split()
            done.add(2)
            chunk.add()

            def rope_k():
                kr_v = sm[:, :, 0:64]
                chain(V.tensor_tensor(kr[:, :, :], kr_v, kr_v, MUL))
                chain(V.tensor_reduce(ss_kr[:, :], kr[:, :, :], AX.X, ADD))
                dve.wait_ge(trig, 2)
                gk = par[:, PARAMS["k_rope_g"]].unsqueeze(1).to_broadcast([P, TT, 64])
                chain(V.tensor_tensor(kr_v, kr_v, gk, MUL))
                x1, x2, d1, d2 = sm[:, :, 0:32], sm[:, :, 32:64], kr[:, :, 0:32], kr[:, :, 32:64]
                V.tensor_tensor(d1, x1, cos[:, :, :], MUL)
                chain(V.tensor_tensor(d2, x2, sin[:, :, :], MUL))
                chain(V.tensor_tensor(d1, d1, d2, SUB))
                V.tensor_tensor(d2, x2, cos[:, :, :], MUL)
                chain(V.tensor_tensor(x1, x1, sin[:, :, :], MUL))
                chain(V.tensor_tensor(d2, d2, x1, ADD))

            def gates_slot(j):
                if j == 0:
                    dve.wait_ge(pow_done, 1)
                    dve.wait_ge(small_t, 1)
                    for t in range(TT):
                        last = V.tensor_scalar(sm[:, t, :], bank_b[:, t * P:t * P + 80], inv1[:, t:t + 1], None, MUL)
                    chain(last)
                    bias = par[:, PARAMS["gate_b"]].unsqueeze(1).to_broadcast([P, TT, 16])
                    chain(V.tensor_tensor(sm[:, :, 64:80], sm[:, :, 64:80], bias, ADD))
                    V.scalar_tensor_tensor(lf[:, :, :], sm[:, :, 72:80], -1.0, sm[:, :, 72:80], MUL, MIN).then_inc(gate_in, 1)
                if j == 1:
                    dve.wait_ge(gate_ln, 1)
                    V.scalar_tensor_tensor(lf[:, :, :], sm[:, :, 72:80], 0.0, lf[:, :, :], MIN, SUB).then_inc(lf_ready, 1)
                if j == 2:
                    dve.wait_ge(f_sum, 1)
                    chain(V.tensor_copy(f_nat[:, :, :], bank_a[:, 0:16].rearrange("p (t h) -> p t h", t=2)))
                    V.tensor_tensor(a_nat[:, :, :], sm[:, :, 64:72], f_nat[:, :, :], SUB).then_inc(a_ready, 1)
                if j == 3:
                    dve.wait_ge(a_row, 1)
                    dve.wait_ge(pool_init, 3)
                    chain(V.tensor_copy(mrow[:, 0, P:P + TOK], bank_b[0:8, 0:TOK]))
                if 3 <= j <= 5:
                    for n in ((0, 1), (2, 3, 4), (5, 6, 7))[j - 3]:
                        a, b = mrow[:, n % 2, :], mrow[:, (n + 1) % 2, :]
                        chain(V.tensor_tensor(b[:, P:P + TOK], a[:, P:P + TOK], a[:, P - 2 ** n:P + TOK - 2 ** n], MAX))
                if j == 5:
                    V.tensor_scalar(m_fin[:, :], mrow[:, 0, P:P + TOK], 0.0, None, MAX).then_inc(m_row, 1)
                if j == 7:
                    dve.wait_ge(m_col, 1)
                    V.tensor_tensor(expm[:, :, :], f_nat[:, :, :], bank_a[:, 16:32].rearrange("p (t h) -> p t h", t=2),
                                    ADD).then_inc(m_sum, 1)

            acc = [stg2[:, j, :] for j in range(2)]
            sgm = [z2[:, 0, j * CW:(j + 1) * CW] for j in range(2)]
            cw = PARAMS["conv_w"].start

            def conv_slot(j, i):
                if j in (1, 3):
                    j //= 2
                    wait(dve, qk_ready, 2 * i)
                    dve.wait_ge(t_done, tr.at(1))
                    b = tbank[tr.n % 2]
                    tr.add()
                    for n in range(4):
                        for f in range(2):
                            ft = 4 * i + 2 * j + f
                            w = par[:, cw + 4 * ft + 3 - n:cw + 4 * ft + 4 - n]
                            dst, src = acc[j][:, f * TOK:(f + 1) * TOK], b[:, f * TOK:(f + 1) * TOK]
                            if n == 0:
                                last = V.tensor_scalar(dst, src, w, None, MUL)
                            else:
                                last = V.scalar_tensor_tensor(dst[:, n:TOK], src[:, 0:TOK - n], w, dst[:, n:TOK], MUL, ADD)
                            if n < 3:
                                last.then_inc(dve_seq, 1)
                                seq.add()
                        if n < 3:
                            dve.wait_ge(dve_seq, seq.at())
                    last.then_inc(conv_done, 1)
                    dve.wait_ge(conv_done, 2 * i + j + 1)
                    dve.sem_inc(t_by_dve, 1)
                elif j in (5, 6):
                    g = j - 5
                    dve.wait_ge(conv_sig, 2 * i + g + 1)
                    V.tensor_tensor(qk_t[:, 4 * i + 2 * g:4 * i + 2 * g + 2, :].rearrange("p a b -> p (a b)"), acc[g], sgm[g],
                                    MUL).then_inc(qk_ready, 1)

            pieces(slot=gates_slot)
            chunk.add()
            for i in range(4):
                pieces(slot=lambda j: conv_slot(j, i))
                chunk.add()
            for i in range(3):
                def slot(j, i=i):
                    if i == 0 and j in (1, 5):
                        if j == 1:
                            dve.wait_ge(early_ready, 16)
                        angles(j // 4)
                    if i == 1 and j == 6:
                        rope_k()
                pieces(slot=slot)
                chunk.add()
            tiles = Tally()
            with loop(dve, 4, {piece: 16, done: 16, chunk: 2, tiles: 2, seq: 2}) as i:
                pieces()
                chunk.add()
                pieces()
                for t, b in enumerate(banks()):
                    tiles.add()
                    dve.wait_ge(sig, tiles.at())
                    chain(V.tensor_tensor(stg2[:, t, :], stg2[:, t, :], stg[:, t, :], MUL))
                    V.scalar_tensor_tensor(nat[:, t, bass.ds(i * CW, CW)], b[:, :], inv1[:, t:t + 1], stg2[:, t, :], MUL,
                                           MUL).then_inc(gated, 1)
                    dve.wait_ge(gated, tiles.at(2))
                    dve.sem_inc(proj_read, 1)
            with loop(dve, 2, {piece: 16, done: 16, chunk: 2, tiles: 4}) as i:
                for c in range(2):
                    pieces()
                    for t, b in enumerate(banks()):
                        tiles.add()
                        dve.wait_ge(sig, tiles.at())
                        V.scalar_tensor_tensor(z1[:, t, bass.ds(i * (2 * CW) + c * CW, CW)], b[:, :], inv1[:, t:t + 1],
                                               stg[:, t, :], MUL, MUL).then_inc(gated, 1)
                        dve.wait_ge(gated, tiles.at(2))
                        dve.sem_inc(proj_read, 1)
            dve.sem_inc(z_full, 1)
            for i in range(2):
                def lat_slot(j, i=i):
                    if i and 1 <= j <= 2:
                        low(lat_hi, lat_lo, 2 * (j - 1), "q_lat_g", 2 * (j - 1))
                pieces(slot=lat_slot)
                chunk.add()

            mask = cst[:, CONSTS["ml_mask"]]
            dve.wait_ge(cst_ready, 16)
            for h in range(H_A):
                def slot(j, h=h):
                    if h == 0 and 1 <= j <= 2:
                        low(lat_hi, lat_lo, 2 + 2 * j, "kv_lat_g", 2 * (j - 1))
                    if h == 0 and j == 0:
                        dve.wait_ge(sumsq, 6)
                        mean(ms_l[:, :, :], ss_l[:, :, :], LORA)
                    e, pt = stg2[:, 0, 0:384], stg2[:, 1, 0:384]
                    if j == 1:
                        dve.wait_ge(ml_s, h + 1)
                        V.scalar_tensor_tensor(e[:, 0:TOK], bank_b[:, 0:TOK], a_nat[:, 0, h:h + 1], mask, SUB,
                                               MAX).then_inc(ml_e, 1)
                        V.scalar_tensor_tensor(e[:, TOK:384], bank_b[:, P:TOK], a_nat[:, 1, h:h + 1], mask[:, 0:P], SUB,
                                               MAX).then_inc(ml_e, 1)
                    if j == 2:
                        dve.wait_ge(ml_w, h + 1)
                        V.scalar_tensor_tensor(pt, bank_a[:, 0:384], DK_A ** -0.5, e, MUL, MUL).then_inc(ml_p, 1)
                    if j == 4:
                        dve.wait_ge(ml_q, 2 * h + 2)
                        if h == 0:
                            dve.wait_ge(m_exp, 1)
                        for t, b in enumerate((bank_b, bank_a)):
                            V.tensor_scalar(ml_t[:, t:t + 1], b[:, DV_A:DV_A + 1], -1.0, None, MUL).then_inc(dve_seq, 1)
                            seq.add()
                        dve.wait_ge(dve_seq, seq.at())
                        for t, b in enumerate((bank_b, bank_a)):
                            chain(V.scalar_tensor_tensor(ml_r[:, t:t + 1], b[:, DV_A:DV_A + 1], expm[:, t, h:h + 1],
                                                         ml_t[:, t:t + 1], MAX, MAX))
                        chain(V.reciprocal(ml_r[:, :], ml_r[:, :]))
                        chain(V.tensor_tensor(ml_t[:, :], ml_r[:, :], ml_r[:, :], MUL))
                        chain(V.tensor_tensor(ml_t[:, :], ml_t[:, :], ml_ss[:, :], MUL))
                        mean(ml_ms[:, :], ml_t[:, :], DV_A)
                    if j == 5:
                        dve.wait_ge(pow_done, 3 + h)
                        chain(V.tensor_tensor(ml_r[:, :], ml_f[:, :], ml_r[:, :], MUL))
                        for t, b in enumerate((bank_b, bank_a)):
                            o = nat[:, t, h * DV_A:(h + 1) * DV_A]
                            last = V.scalar_tensor_tensor(o, b[:, 0:DV_A], ml_r[:, t:t + 1], o, MUL, MUL)
                        last.then_inc(ml_done, 1)
                pieces(slot=slot)
                chunk.add()

            dve.wait_ge(w_used, done.at(RING))
            gq = [par[:, PARAMS["q_rope_g"]][:, 32 * i:32 * i + 32].unsqueeze(1).to_broadcast([P, TT, 32]) for i in range(2)]
            for i in range(2):
                V.tensor_tensor(cos_g[:, :, 32 * i:32 * i + 32], cos[:, :, :], gq[i], MUL)
                last = V.scalar_tensor_tensor(sin_g[:, :, 32 * i:32 * i + 32], sin[:, :, :], (-1.0, 1.0)[i], gq[1 - i], MUL, MUL)
            chain(last)
            n_squares = Tally()

            def latent_behind(c, j):
                if c == 0 or j > 1:
                    return
                if j == 0 and c > 1 and LATENT[c - 2][0] == "r":
                    m = int(LATENT[c - 2][1])
                    V.tensor_tensor(roped_of[m][:, :, :], roped_of[m][:, :, :], rope_b[:, :, :], ADD).then_inc(roped, 1)
                name = LATENT[c - 1]
                kind, m = name[0], int(name[1])
                if kind == "v":
                    return
                x, sq = x_of[name], squares_of[name]
                if j == 0:
                    dve.wait_ge(proj_read, chunk.at() * 2)
                    width = D_ROPE if kind == "r" else D_NOPE
                    n = CW // width
                    if kind == "q":
                        for t in range(TT):
                            last = V.tensor_tensor(sq[:, t, :], x[:, t, :], x[:, t, :], MUL)
                        chain(last)
                    dst = {"r": ss_qr, "q": ss_q, "k": ss_k}[kind][:, :, 0 if kind == "k" else n * m:][:, :, 0:n]
                    for t in range(TT):
                        last = V.tensor_reduce(dst[:, t, :], sq[:, t, :].rearrange("p (h d) -> p h d", d=width), AX.X, ADD)
                    n_squares.add()
                    last.then_inc(squared, 1)
                    dve.wait_ge(squared, n_squares.at())
                if j == 0 and kind == "q":
                    V.scalar_tensor_tensor(dst, dst, D_HQK * EPS, ss_qr[:, :, 4 * m:4 * m + 4], ADD, ADD).then_inc(pow_asked, 1)
                if j == 0 and kind == "k":
                    for t in range(TT):
                        last = V.tensor_scalar(ss_k[:, t, :], ss_k[:, t, :], ss_kr[:, t:t + 1], None, ADD)
                    chain(last)
                    mean(ss_k[:, :, :], ss_k[:, :, :], D_HQK)
                if j == 1 and kind == "r":
                    heads = lambda buf, t: buf[:, t, :].rearrange("p (h d) -> p h d", d=D_ROPE)
                    table = lambda tab, t, lo, hi: tab[:, t, lo:hi].unsqueeze(1).to_broadcast([P, 8, hi - lo])
                    wait(dve, roped, m)
                    for t in range(TT):
                        xs, b = heads(x, t), heads(rope_b, t)
                        V.tensor_tensor(heads(roped_of[m], t), xs, table(cos_g, t, 0, 64), MUL)
                        V.tensor_tensor(b[:, :, 0:32], xs[:, :, 32:64], table(sin_g, t, 0, 32), MUL)
                        last = V.tensor_tensor(b[:, :, 32:64], xs[:, :, 0:32], table(sin_g, t, 32, 64), MUL)
                    chain(last)
                if j == 1 and kind == "k":
                    dve.wait_ge(pow_done, (11, 12, 13, 15)[m])
                    for t in range(TT):
                        ks = x[:, t, :].rearrange("p (h d) -> p h d", d=D_NOPE)
                        ik = inv_k[:, t, :].unsqueeze(2)
                        V.tensor_tensor(ks, ks, ik.to_broadcast([P, 4, D_NOPE]), MUL)
                        last = V.tensor_tensor(shared_of[m][:, t, :].rearrange("p (h d) -> p h d", d=D_ROPE),
                                               kr[:, t, :].unsqueeze(1).to_broadcast([P, 4, D_ROPE]),
                                               ik.to_broadcast([P, 4, D_ROPE]), MUL)
                    last.then_inc(k_scaled, 1)

            def latent_slot(c, j):
                latent_behind(c, j)
                for kind, m, part in LATENT_GROUPS[c, j]:
                    if kind == "a":
                        low(a_hi, a_lo, 2 * part, "ml_g", 2 * part)
                    else:
                        tr.add()

            def finish_head(h, n, dst, gate):
                dve.wait_ge(o_done, n + 1)
                chain(V.reciprocal(rden[:, :], den[:, h % 2, :]))
                for t in range(TT):
                    o, b = dst[:, t, h * P:(h + 1) * P], bank_b[:, t * P:(t + 1) * P]
                    if gate:
                        last = V.scalar_tensor_tensor(o, b, rden[:, t:t + 1], o, MUL, MUL)
                    else:
                        last = V.tensor_scalar(o, b, rden[:, t:t + 1], None, MUL)
                last.then_inc(o_read, 1)

            def turn_tail(j, g=None):
                if 1 <= j <= 6:
                    low(a_hi, a_lo, 2 * (j - 1), g, 2 * (j - 1))

            def turn_head(j, g=None):
                if 2 <= j <= 3:
                    low(a_hi, a_lo, 2 * (j + 4), g, 2 * (j + 4))

            def heads_b(n):
                h, odd = divmod(n, 2)
                if not odd:
                    if h >= 0:
                        tr.add()
                    h += 1
                    if h == H_B:
                        return
                    s = stg[:, h % 2, 0:384]
                    dve.wait_ge(s_done, h + 1)
                    if h > 1:
                        dve.wait_ge(o_done, h - 1)
                    V.tensor_tensor(s, bank_a[:, 0:384], cst[:, CONSTS["attn_mask"]], ADD).then_inc(s_read, 1)
                    dve.wait_ge(s_read, h + 1)
                    V.tensor_reduce(nmax[:, h % 2, 0:1], s[:, 0:P], AX.X, MAX, negate=True).then_inc(dve_seq, 1)
                    seq.add()
                    chain(V.tensor_reduce(nmax[:, h % 2, 1:2], s[:, P:384], AX.X, MAX, negate=True))
                    if h % 4 == 0:
                        dve.wait_ge(pow_done, (14, 16, 17, 18)[h // 4])
                    V.tensor_tensor(nb[:, h % 2, :], nmax[:, h % 2, :], inv_q[:, :, h], MUL).then_inc(b_ready, 1)
                elif h >= 0:
                    if h % 4 == 0:
                        dve.wait_ge(yb_in[h // 4], 16)
                    finish_head(h, h, yb, True)

            for c in range(len(LATENT)):
                def slot(j, c=c):
                    latent_slot(c, j)
                    if c == 13:
                        heads_b(j - 2)
                pieces(NORM_LORA, slot=slot)
                if LATENT[c][0] == "v":
                    m = int(LATENT[c][1])
                    if m == 0:
                        dve.wait_ge(z_out, 16 * 6)
                    dve.wait_ge(proj_read, chunk.n * 2)
                    V.tensor_scalar(v_b[:, 0, m * CW:(m + 1) * CW], banks()[0][:, :], inv_l[:, 1, 0:1], None,
                                    MUL).then_inc(proj_read, 1)
                else:
                    chunk.add()
            for c in range(4):
                def slot(j, c=c):
                    if c == 0:
                        latent_slot(14, j)
                    heads_b(8 * c + j)
                    if c == 3:
                        turn_tail(j)
                pieces(slot=slot)
                chunk.add()
            for c in range(4):
                def slot(j, c=c):
                    if c == 0:
                        turn_head(j)
                    if c == 3:
                        turn_tail(j)
                    if j == 7:
                        for t in range(TT):
                            y = nat[:, t, c * CW:(c + 1) * CW]
                            dve.wait_ge(sig, 8 + 8 + 4 * c + 2 * t + 2)
                            V.tensor_tensor(y, y, stg[:, t, :], MUL).then_inc(dve_seq, 1)
                            seq.add()
                pieces(slot=slot)
                for t, b in enumerate(banks()):
                    y = nat[:, t, c * CW:(c + 1) * CW]
                    V.tensor_tensor(stg2[:, t, :], b[:, :], stg2[:, t, :], MUL).then_inc(proj_read, 1)
                    dve.wait_ge(proj_read, chunk.at(-1) * 2 + t + 1)
                    dve.wait_ge(dve_seq, seq.at())
                    V.tensor_tensor(y, y, stg2[:, t, :], ADD).then_inc(gated, 1)

            def add_chunk(c, other):
                for t, b in enumerate(banks()):
                    o = nat[:, t, c * CW:(c + 1) * CW]
                    V.tensor_tensor(o, b[:, :], other[:, t, c * CW:(c + 1) * CW], ADD).then_inc(res_ready, 1)
                    res.add()
                    dve.wait_ge(res_ready, res.at())
                    dve.sem_inc(proj_read, 1)

            res = Tally()
            for c in range(4):
                pieces(slot=turn_head if c == 0 else (lambda j: turn_tail(j, "mix_g")) if c == 3 else None)
                if c == 0:
                    dve.wait_ge(x_again, 16)
                add_chunk(c, yb)

            def mean_of_chunks(n):
                dve.wait_ge(sumsq, n)
                chain(V.tensor_reduce(ss1[:, :], ss2[:, :, :], AX.X, ADD))
                mean(ms1[:, :], ss1[:, :], D)

            def in2_slot(j):
                turn_head(j, "mix_g")
                if j == 4:
                    mean_of_chunks(6 + 8)
            pieces(slot=in2_slot)
            chunk.add()

            def heads_2(n):
                h, odd = divmod(n, 2)
                if not odd:
                    if h >= 0:
                        tr.add()
                    h += 1
                    if h == H_2:
                        return
                    n = H_B + h
                    s = stg[:, h % 2, :]
                    if h == 0:
                        dve.wait_ge(alibi_in_s, 16)
                    dve.wait_ge(s_done, n + 1)
                    if h > 1:
                        dve.wait_ge(o_done, n - 1)
                    V.scalar_tensor_tensor(s, bank_a[:, :], HD_2 ** -0.5, alibi[:, h, :], MUL, ADD).then_inc(s_read, 1)
                    dve.wait_ge(s_read, n + 1)
                    V.tensor_reduce(nmax[:, h % 2, :], s.rearrange("p (t k) -> p t k", t=2), AX.X, MAX,
                                    negate=True).then_inc(b_ready, 1)
                elif h >= 0:
                    finish_head(h, H_B + h, y2, False)

            for i in range(1, 6):
                pieces(slot=(lambda j: heads_2(j - 8) if j >= 6 else None) if i == 5 else None)
                chunk.add()
                if i < 5:
                    tr.add(2)
            for c in range(2):
                def slot(j, c=c):
                    heads_2(8 * c + j)
                    if c and j >= 5:
                        low(a_hi, a_lo, 2 * (j - 5))
                pieces(slot=slot)
                chunk.add()
            def mapped(g):
                dve.wait_ge(f_hi, g + 1)
                k = slice(8 + 2 * g, 10 + 2 * g)
                V.tensor_tensor(a_lo[:, k, :].rearrange("p a b -> p (a b)"), bank_b[:, :],
                                a_hi[:, k, :].rearrange("p a b -> p (a b)").bitcast(f32), SUB).then_inc(f_lo, 1)

            for g in range(FG):
                dve.wait_ge(f_r, g + 1)
                wait(dve, f_y, g)
                both = bank_a[:, :].rearrange("p (c k) -> p c k", c=2)
                a, b = both[:, :, 0:N_COS], both[:, :, N_COS:FD]
                chain(V.tensor_copy(cos_part[:, :, :], a))
                a = cos_part[:, :, 1:FD // 2]
                V.tensor_tensor(re_sb[:, :, 1:FD // 2], a, b, SUB)
                V.tensor_tensor(re_sb[:, :, FD - 1:FD // 2:-1], a, b, ADD)
                V.tensor_copy(re_sb[:, :, 0:FD:FD // 2], cos_part[:, :, 0:N_COS:FD // 2]).then_inc(f_re, 1)
                dve.wait_ge(f_re, g + 1)
                if g == 2:
                    low(a_hi, a_lo, 6)
                if g + 1 < FG:
                    mapped(g)
            for c in range(4):
                pieces(slot=(lambda j: mapped(FG - 1) if j == 0 else None) if c == 0 else
                       (lambda j: turn_tail(j, "mlp_g")) if c == 3 else None)
                add_chunk(c, nat)
            def slab(first=False, end=False):
                for c in range(8):
                    def slot(j, c=c):
                        if end and c > 4 and j == 4:
                            n = c - 5
                            dve.wait_ge(fg_in_s, 16)
                            dve.wait_ge(sumsq, 22 + 2 * (n + 1))
                            y = nat[:, :, n * CW:(n + 1) * CW]
                            V.tensor_tensor(y, y, fg[:, n * CW:(n + 1) * CW].unsqueeze(1).to_broadcast([P, TT, CW]),
                                            MUL).then_inc(weighted, 1)
                        if 1 <= c <= 4 and 1 <= j <= 2:
                            low(m_hi, m_lo, 4 * (c - 1) + 2 * (j - 1))
                        if first and c == 0:
                            turn_head(j, "mlp_g")
                            if j == 4:
                                mean_of_chunks(14 + 8)
                    pieces(slot=slot)
                    if c < 4:
                        chunk.add()
                        for t in range(TT):
                            dve.wait_ge(proj_read, chunk.at(-1) * 2 + t + 1)
                            V.tensor_tensor(stg[:, t, :], stg[:, t, :], stg[:, t, :], MUL).then_inc(relu, 1)
                    else:
                        add_chunk(c - 4, nat)
            slab(first=True)
            with loop(dve, N_SLABS - 2, {piece: 64, done: 64, chunk: 8, tr: 8, his: 8, res: 8}):
                slab()
            slab(end=True)
            mean_of_chunks(22 + 8)
            dve.wait_ge(pow_done, 21)
            dve.wait_ge(weighted, 3)
            for t, c in ((0, 0), (0, 1), (0, 2), (0, 3), (1, 3)):
                y, weight = nat[:, t, c * CW:(c + 1) * CW], fg[:, c * CW:(c + 1) * CW]
                if c < 3:
                    V.tensor_scalar(y, y, inv4[:, t:t + 1], None, MUL).then_inc(out_ready, 1)
                else:
                    V.scalar_tensor_tensor(y, y, inv4[:, t:t + 1], weight, MUL, MUL).then_inc(out_ready, 1)


def _units(w):
    k, n = w.shape
    v = w.reshape(k // 512, 4, P, n // CW, CW).transpose(3, 0, 2, 1, 4)
    return v.reshape(-1, P, 4 * CW)


def _stream(i):
    s = np.cumsum([0, 1024, 1024, 2048, 2048, 8, 8, 2048, 512, 512, 64, 2048, 2048, 2048])
    w = i["w_in"][0]
    q, k, v, o, gi, gf, z, cq, ckv, kr, zb, ga, gb = (w[:, s[n]:s[n + 1]] for n in range(13))
    parts = []
    small = np.concatenate([kr, gi, gf, np.zeros((D, P - 80), w.dtype)], axis=1)
    parts.append(small.reshape(KT, P, P).transpose(1, 0, 2).reshape(1, P, KT * P))
    parts += [_units(q), _units(k), _units(v)]
    for c in range(4):
        parts += [_units(o[:, c * CW:(c + 1) * CW]), _units(z[:, c * CW:(c + 1) * CW])]
    parts += [_units(zb), _units(cq), _units(ckv), _units(ga), _units(gb)]
    latent = {}
    uq = i["w_uq"][0].reshape(LORA, H_B, D_HQK)
    ukv = i["w_ukv"][0].reshape(LORA, H_B, D_NOPE + 128)
    for kind, part in (("q", uq[:, :, :D_NOPE]), ("r", uq[:, :, D_NOPE:]), ("k", ukv[:, :, :D_NOPE]),
                       ("v", ukv[:, :, D_NOPE:])):
        latent[kind] = _units(part.reshape(LORA, -1))
    parts += [latent[name[0]][int(name[1]):int(name[1]) + 1] for name in LATENT]
    parts += [_units(i["w_a"][0]), _units(i["w_b"][0]), _units(i["w_out"][0])]
    w2 = i["w_in_2"][0]
    parts += [_units(w2[:, 1024:]), _units(w2[:, :1024]), _units(np.concatenate([i["w_out_2"][0][1024:], i["w_out_2"][0][:1024]], axis=0))]
    for n in range(N_SLABS):
        parts.append(_units(i["w_up_2"][0][:, n * D:(n + 1) * D]))
        parts.append(_units(i["w_down_2"][0][n * D:(n + 1) * D, :]))
    r = np.concatenate(parts, axis=0)
    assert r.shape == (UNITS, P, 2 * PIECE), r.shape
    return r


def _params(i):
    r = np.zeros((P, N_PARAMS), np.float32)
    col = lambda v: v.reshape(-1, P).T
    for name, v in (("norm_g", col(i["norm_g"][0])), ("ml_g", col(i["mlstm_norm_g"][0])),
                    ("q_lat_g", col(i["q_lat_g"][0])), ("kv_lat_g", col(i["kv_lat_g"][0])),
                    ("q_nope_g", col(i["q_norm_g"][0][:P])), ("k_nope_g", col(i["k_norm_g"][0][:P])),
                    ("mix_g", col(i["norm_mix_g_2"][0])), ("mlp_g", col(i["norm_mlp_g_2"][0])),
                    ("conv_w", i["conv_w"][0].reshape(4, 16, P).transpose(2, 1, 0).reshape(P, 64)),
                    ("gate_b", np.broadcast_to(i["gate_bias"][0], (P, 16))),
                    ("q_rope_g", np.broadcast_to(i["q_norm_g"][0][P:], (P, 64))),
                    ("k_rope_g", np.broadcast_to(i["k_norm_g"][0][P:], (P, 64)))):
        r[:, PARAMS[name]] = v
    return r


def _consts():
    early = np.zeros((P, N_EARLY), np.float32)
    r = np.zeros((P, N_CONSTS), np.float32)
    n = np.arange(P)
    r[:, CONSTS["ident"]] = np.eye(P)
    ahead = np.where(n[None, :] > n[:, None], -BIG, 0.0)
    r[:, CONSTS["attn_mask"]] = np.concatenate([ahead, np.zeros((P, P)), ahead], axis=1)
    r[:, CONSTS["ml_mask"]] = np.concatenate([np.where(n[:, None] > n[None, :], BIG, 0.0), np.zeros((P, P))], axis=1)
    early[:, EARLY["tri"]] = n[:, None] <= n[None, :]
    early[:, EARLY["ones"]] = 1.0
    e = (np.float32(-np.log(10000.0)) * np.arange(0, D_ROPE, 2, dtype=np.float32)) / np.float32(D_ROPE)
    early[:, EARLY["inv_freq"]] = np.exp(e.astype(np.float64)).astype(np.float32)
    m = np.arange(FD)
    ang = 2 * np.pi * ((m[:, None] * m[None, :]) % FD) / FD
    dft = np.concatenate([np.cos(ang)[:, :N_COS], np.sin(ang)[:, 1:N_COS - 1], np.cos(ang), np.sin(ang)],
                         axis=1).astype(np.float32)
    dft = dft.reshape(2, P, 3 * FD).transpose(1, 0, 2).copy()
    t = np.arange(TOK)
    dist = np.abs(t[:, None] - t[None, :])
    seen = np.zeros((TOK, TOK))
    for window, dil in ((128, 1), (512, 4), (2048, 16)):
        seen += (dist % dil == 0) & (dist // dil <= window // 2 // dil)
    table = np.where(seen > 0, np.log(np.maximum(seen, 1)), -BIG)
    slopes = 2.0 ** (-8.0 * (np.arange(H_2) + 1) / H_2)
    alibi = (table[None] - slopes[:, None, None] * dist[None]).astype(np.float32)
    alibi = alibi.reshape(H_2, 2, P, TOK).transpose(2, 0, 1, 3).reshape(P, H_2, 2 * TOK).copy()
    return r, early, dft, alibi


def kernel(**inputs):
    import concourse.bacc as bacc
    from concourse.bass_utils import run_bass_kernel_spmd

    i = {k: np.asarray(v) for k, v in inputs.items()}
    consts, early, dft, alibi = _consts()
    arrays = {
        "stream": _stream(i),
        "x": np.ascontiguousarray(i["x"][0]),
        "consts": consts,
        "early": early,
        "params": _params(i),
        "pos": np.ascontiguousarray(i["positions"][0].reshape(TT, P).T),
        "dft": dft,
        "alibi": alibi,
        "fg": np.ascontiguousarray(np.broadcast_to(i["norm_final_g_2"], (P, D))),
        "wf": np.ascontiguousarray(i["w_fourier_2"][0].reshape(FG, 2, P, FD).transpose(2, 0, 1, 3)),
    }
    nc = bacc.Bacc("TRN2", target_bir_lowering=False, num_devices=1)
    f32 = mybir.dt.float32
    ap = {n: nc.dram_tensor(n, a.shape, mybir.dt.from_np(a.dtype), kind="ExternalInput").ap() for n, a in arrays.items()}
    stores = [nc.dram_tensor(n, (P, TT, D), f32, kind="Internal").ap() for n in ("z_store", "ga_store", "gb_store")]
    out = nc.dram_tensor("out", (TOK, D), f32, kind="ExternalOutput").ap()
    build(nc, *(ap[n] for n in ("stream", "x", "consts", "early", "params", "pos", "dft", "alibi", "fg", "wf")), *stores, out)
    r = run_bass_kernel_spmd(nc, [arrays], core_ids=[0])
    return r.results[0]["out"].reshape(1, TOK, D)
```
